# Optimizing a Trainium2 kernel written in Bass

```python
import math
import jax, jax.numpy as jnp
from jax import lax
import numpy as np

D_MODEL = 1024
BATCH = 1
SEQ = 512
DEPTH = 1

N_META = 16
ATT_HEADS = 4
ATT_HEAD_DIM = 64
ATT_V_DIM = 2 * ATT_HEAD_DIM
REC_HEADS = 4
REC_DK = 128
REC_DV = 128
ATT_WIDTH = ATT_HEADS * ATT_V_DIM
REC_WIDTH = REC_HEADS * REC_DV
MIX_WIDTH = ATT_WIDTH + REC_WIDTH
COL_SIZES = (
    ATT_HEADS * 2 * ATT_HEAD_DIM,
    ATT_HEADS * 2 * ATT_HEAD_DIM,
    ATT_WIDTH,
    REC_HEADS * REC_DK,
    REC_HEADS * REC_DK,
    REC_WIDTH,
    REC_WIDTH,
)
IN_COLS = sum(COL_SIZES)
SPLIT_POINTS = tuple(int(v) for v in np.cumsum(COL_SIZES)[:-1])
Q_BLOCK = 128
REC_CHUNK = 64
ROPE_THETA = 10000.0
PEER_HEADS = 8
PEER_QUERY_DIM = 256
N_KEYS = 128
N_EXPERTS = N_KEYS * N_KEYS
PEER_TOPK = 16
PEER_BLOCK = 128
EPS = 1e-6


def rmsnorm(x, w):
    xf = x.astype(jnp.float32)
    y = xf * lax.rsqrt(jnp.mean(xf * xf, axis=-1, keepdims=True) + EPS)
    return (y * w.astype(jnp.float32)).astype(x.dtype)

def rope_tables(T, d):
    inv_freq = ROPE_THETA ** (-jnp.arange(0, d, 2, dtype=jnp.float32) / d)
    ang = jnp.arange(T, dtype=jnp.float32)[:, None] * inv_freq[None, :]
    ang = jnp.concatenate([ang, ang], axis=-1)
    return jnp.cos(ang), jnp.sin(ang)

def apply_rope(z, cos, sin):
    half = z.shape[-1] // 2
    rot = jnp.concatenate([-z[..., half:], z[..., :half]], axis=-1)
    return (z * cos.astype(z.dtype) + rot * sin.astype(z.dtype)).astype(z.dtype)

def lambda_init(layer_idx):
    return 0.8 - 0.6 * math.exp(-0.3 * layer_idx)

def diff_attention(aq, ak, av, lq1, lk1, lq2, lk2, subln_w, lam_init, cos, sin):
    B, T, _ = aq.shape
    q = apply_rope(aq.reshape(B, T, ATT_HEADS, 2, ATT_HEAD_DIM).transpose(3, 0, 2, 1, 4), cos, sin)
    k = apply_rope(ak.reshape(B, T, ATT_HEADS, 2, ATT_HEAD_DIM).transpose(3, 0, 2, 1, 4), cos, sin)
    v = av.reshape(B, T, ATT_HEADS, ATT_V_DIM).transpose(0, 2, 1, 3)
    q = q * (ATT_HEAD_DIM ** -0.5)
    lam = (jnp.exp(jnp.sum(lq1.astype(jnp.float32) * lk1.astype(jnp.float32)))
           - jnp.exp(jnp.sum(lq2.astype(jnp.float32) * lk2.astype(jnp.float32))) + lam_init)
    neg = jnp.finfo(jnp.float32).min

    def block(q_blk, k_blk, v_blk, q_start):
        nq, nk = q_blk.shape[-2], k_blk.shape[-2]
        mask = jnp.arange(nk)[None, :] <= (q_start + jnp.arange(nq))[:, None]
        s = jnp.einsum('pbhqd,pbhkd->pbhqk', q_blk, k_blk).astype(jnp.float32)
        p = jax.nn.softmax(jnp.where(mask, s, neg), axis=-1)
        w = p[0] - lam * p[1]
        return jnp.einsum('bhqk,bhkv->bhqv', w.astype(v_blk.dtype), v_blk)

    outs = [block(q[..., :N_META, :], k[..., :N_META, :], v[:, :, :N_META], 0)]
    for i in range((T - N_META) // Q_BLOCK):
        s0 = N_META + i * Q_BLOCK
        e0 = s0 + Q_BLOCK
        outs.append(block(q[..., s0:e0, :], k[..., :e0, :], v[:, :, :e0], s0))
    o = jnp.concatenate(outs, axis=2)
    o = rmsnorm(o, subln_w) * (1.0 - lam_init)
    return o.transpose(0, 2, 1, 3).reshape(B, T, ATT_WIDTH)

def gla_chunk(S, q, k, v, g):
    C = q.shape[2]
    cum = jnp.cumsum(g, axis=2)
    inter = jnp.einsum('bhtc,bhcv->bhtv', q * jnp.exp(cum), S)
    causal = jnp.tril(jnp.ones((C, C), dtype=bool))[:, :, None]
    diff = cum[:, :, :, None, :] - cum[:, :, None, :, :]
    decay = jnp.where(causal, jnp.exp(jnp.where(causal, diff, 0.0)), 0.0)
    A = jnp.einsum('bhtc,bhsc,bhtsc->bhts', q, k, decay)
    intra = jnp.einsum('bhts,bhsv->bhtv', A, v)
    last = cum[:, :, -1]
    S_new = (jnp.exp(last)[..., None] * S
             + jnp.einsum('bhsc,bhsv->bhcv', k * jnp.exp(last[:, :, None, :] - cum), v))
    return S_new, inter + intra

def hgrn2(rq, rf, ri, rg, lb, norm_w):
    B, T, _ = rq.shape

    def heads(z, d):
        return z.reshape(B, T, REC_HEADS, d).transpose(0, 2, 1, 3).astype(jnp.float32)

    q = jax.nn.silu(heads(rq, REC_DK))
    lbh = lb.reshape(REC_HEADS, 1, REC_DK)
    f = lbh + (1.0 - lbh) * jax.nn.sigmoid(heads(rf, REC_DK))
    k = 1.0 - f
    g = jnp.log(f)
    v = heads(ri, REC_DV)
    S0 = jnp.zeros((B, REC_HEADS, REC_DK, REC_DV), jnp.float32)
    S_meta, o_meta = gla_chunk(S0, q[:, :, :N_META], k[:, :, :N_META], v[:, :, :N_META], g[:, :, :N_META])
    n_chunks = (T - N_META) // REC_CHUNK

    def to_chunks(z):
        z = z[:, :, N_META:].reshape(B, REC_HEADS, n_chunks, REC_CHUNK, z.shape[-1])
        return z.transpose(2, 0, 1, 3, 4)

    _, o_real = lax.scan(lambda S, xs: gla_chunk(S, *xs), S_meta,
                         (to_chunks(q), to_chunks(k), to_chunks(v), to_chunks(g)))
    o_real = o_real.transpose(1, 2, 0, 3, 4).reshape(B, REC_HEADS, T - N_META, REC_DV)
    o = jnp.concatenate([o_meta, o_real], axis=2)
    o = rmsnorm(o, norm_w[:, None, :])
    o = o.transpose(0, 2, 1, 3).reshape(B, T, REC_WIDTH) * jax.nn.silu(rg.astype(jnp.float32))
    return o.astype(rq.dtype)

def token_mix(a, w_in, lb, rec_norm_w, lq1, lk1, lq2, lk2, subln_w, w_out, lam_init, cos, sin):
    proj = jnp.einsum('btd,dc->btc', a, w_in)
    aq, ak, av, rq, rf, ri, rg = jnp.split(proj, SPLIT_POINTS, axis=-1)
    att = diff_attention(aq, ak, av, lq1, lk1, lq2, lk2, subln_w, lam_init, cos, sin)
    rec = hgrn2(rq, rf, ri, rg, lb, rec_norm_w)
    mixed = jnp.concatenate([att, rec.astype(att.dtype)], axis=-1)
    return jnp.einsum('btc,cd->btd', mixed, w_out)

def peer_ffn(h, w_query, subkeys, u_table, v_table):
    B, T, D = h.shape
    n = B * T
    pad = (-n) % PEER_BLOCK
    blocks = jnp.pad(h.reshape(n, D), ((0, pad), (0, 0))).reshape(-1, PEER_BLOCK, D)

    def one_block(xb):
        q = jnp.einsum('nd,dc->nc', xb, w_query).reshape(PEER_BLOCK, PEER_HEADS, 2, PEER_QUERY_DIM // 2)
        s = jnp.einsum('nhpc,hpkc->nhpk', q, subkeys).astype(jnp.float32)
        sv, si = lax.top_k(s, PEER_TOPK)
        cand_s = (sv[:, :, 0, :, None] + sv[:, :, 1, None, :]).reshape(PEER_BLOCK, PEER_HEADS, PEER_TOPK * PEER_TOPK)
        cand_i = (si[:, :, 0, :, None] * N_KEYS + si[:, :, 1, None, :]).reshape(PEER_BLOCK, PEER_HEADS, PEER_TOPK * PEER_TOPK)
        top_s, pos = lax.top_k(cand_s, PEER_TOPK)
        experts = jnp.take_along_axis(cand_i, pos, axis=-1).reshape(PEER_BLOCK, PEER_HEADS * PEER_TOPK)
        gates = jax.nn.softmax(top_s, axis=-1).reshape(PEER_BLOCK, PEER_HEADS * PEER_TOPK)
        u = u_table[experts]
        hid = jax.nn.gelu(jnp.einsum('nkd,nd->nk', u, xb).astype(jnp.float32), approximate=False) * gates
        return jnp.einsum('nk,nkd->nd', hid.astype(xb.dtype), v_table[experts])

    y = lax.map(one_block, blocks).reshape(-1, D)[:n]
    return y.reshape(B, T, D)

def first_inputs(seed: int = 0) -> dict:
    key = jax.random.key(seed)
    ks = jax.random.split(key, 18)
    nrm = jax.random.normal
    f32 = jnp.float32
    return {
        "x": nrm(ks[0], (BATCH, SEQ, D_MODEL), f32),
        "meta_tokens": nrm(ks[1], (N_META, D_MODEL), f32),
        "mix_norm_w": 1.0 + 0.02 * nrm(ks[2], (DEPTH, D_MODEL), f32),
        "w_in": nrm(ks[3], (DEPTH, D_MODEL, IN_COLS), f32) * D_MODEL ** -0.5,
        "rec_lb_logits": 0.5 * nrm(ks[4], (DEPTH + 1, REC_HEADS * REC_DK), f32),
        "rec_norm_w": 1.0 + 0.02 * nrm(ks[5], (DEPTH, REC_HEADS, REC_DV), f32),
        "diff_lambda_q1": 0.1 * nrm(ks[6], (DEPTH, ATT_HEAD_DIM), f32),
        "diff_lambda_k1": 0.1 * nrm(ks[7], (DEPTH, ATT_HEAD_DIM), f32),
        "diff_lambda_q2": 0.1 * nrm(ks[8], (DEPTH, ATT_HEAD_DIM), f32),
        "diff_lambda_k2": 0.1 * nrm(ks[9], (DEPTH, ATT_HEAD_DIM), f32),
        "diff_subln_w": 1.0 + 0.02 * nrm(ks[10], (DEPTH, ATT_V_DIM), f32),
        "w_out": nrm(ks[11], (DEPTH, MIX_WIDTH, D_MODEL), f32) * MIX_WIDTH ** -0.5,
        "ffn_norm_w": 1.0 + 0.02 * nrm(ks[12], (DEPTH, D_MODEL), f32),
        "peer_w_query": nrm(ks[13], (DEPTH, D_MODEL, PEER_HEADS * PEER_QUERY_DIM), f32) * D_MODEL ** -0.5,
        "peer_subkeys": nrm(ks[14], (DEPTH, PEER_HEADS, 2, N_KEYS, PEER_QUERY_DIM // 2), f32) * (PEER_QUERY_DIM // 2) ** -0.5,
        "peer_u": nrm(ks[15], (DEPTH, N_EXPERTS, D_MODEL), f32) * D_MODEL ** -0.5,
        "peer_v": nrm(ks[16], (DEPTH, N_EXPERTS, D_MODEL), f32) * PEER_HEADS ** -0.5,
        "final_norm_w": 1.0 + 0.02 * nrm(ks[17], (D_MODEL,), f32),
    }

def first_block(x, meta_tokens, mix_norm_w, w_in, rec_lb_logits, rec_norm_w,
              diff_lambda_q1, diff_lambda_k1, diff_lambda_q2, diff_lambda_k2,
              diff_subln_w, w_out, ffn_norm_w, peer_w_query, peer_subkeys,
              peer_u, peer_v, final_norm_w):
    B = x.shape[0]
    T = N_META + x.shape[1]
    meta = jnp.broadcast_to(meta_tokens[None].astype(x.dtype), (B, N_META, D_MODEL))
    h = jnp.concatenate([meta, x], axis=1)
    cos, sin = rope_tables(T, ATT_HEAD_DIM)
    lb_all = jnp.cumsum(jax.nn.softmax(rec_lb_logits.astype(jnp.float32), axis=0), axis=0)
    for l in range(DEPTH):
        a = rmsnorm(h, mix_norm_w[l])
        h = h + token_mix(a, w_in[l], lb_all[l], rec_norm_w[l],
                          diff_lambda_q1[l], diff_lambda_k1[l], diff_lambda_q2[l], diff_lambda_k2[l],
                          diff_subln_w[l], w_out[l], lambda_init(l), cos, sin).astype(h.dtype)
        if l == DEPTH - 1:
            h = h[:, N_META:]
        h = h + peer_ffn(rmsnorm(h, ffn_norm_w[l]), peer_w_query[l], peer_subkeys[l],
                         peer_u[l], peer_v[l]).astype(h.dtype)
    return rmsnorm(h, final_norm_w)


EXPAND = 2
D_MIX = EXPAND * D_MODEL
D_SSD = D_MIX // 2
D_MLA = D_MIX - D_SSD
SSD_HEAD_DIM = 64
SSD_HEADS = D_SSD // SSD_HEAD_DIM
SSD_GROUPS = 2
SSD_HPG = SSD_HEADS // SSD_GROUPS
SSD_STATE = 128
CONV_WIDTH = 4
CHUNK = 128
MLA_HEADS = 8
QK_NOPE = 64
QK_ROPE = 32
QK_DIM = QK_NOPE + QK_ROPE
V_HEAD = D_MLA // MLA_HEADS
Q_LORA = 384
KV_LORA = 256
D_FF = 2816
N_MOD = 9
D_CONV = D_SSD + 2 * SSD_GROUPS * SSD_STATE
IN_WIDTHS = (D_SSD, D_SSD, SSD_GROUPS * SSD_STATE, SSD_GROUPS * SSD_STATE,
             SSD_HEADS, Q_LORA, KV_LORA, QK_ROPE)
D_IN_PROJ = sum(IN_WIDTHS)
IN_SPLITS = tuple(int(v) for v in np.cumsum(IN_WIDTHS)[:-1])


def rmsnorm_2(x, w):
    xf = x.astype(jnp.float32)
    y = xf * lax.rsqrt(jnp.mean(xf * xf, axis=-1, keepdims=True) + EPS)
    return (y * w.astype(jnp.float32)).astype(x.dtype)

def modulate(h, shift, scale):
    return h * (1.0 + scale[:, None, :]) + shift[:, None, :]

def swiglu(h, w_gate, w_up, w_down):
    return (jax.nn.silu(h @ w_gate) * (h @ w_up)) @ w_down

def apply_rope_2(u, cos, sin):
    u1, u2 = jnp.split(u, 2, axis=-1)
    return jnp.concatenate([u1 * cos - u2 * sin, u2 * cos + u1 * sin], axis=-1)

def causal_depthwise_conv(u, w, b):
    out = lax.conv_general_dilated(
        u, w[:, None, :].astype(u.dtype), window_strides=(1,),
        padding=[(CONV_WIDTH - 1, 0)],
        dimension_numbers=('NWC', 'WIO', 'NWC'),
        feature_group_count=u.shape[-1])
    return out + b.astype(u.dtype)

def ssd_chunked(xh, dt, A, Bm, Cm):
    b, S = xh.shape[0], xh.shape[1]
    nc = S // CHUNK
    dtype = xh.dtype
    xdt = (xh * dt[..., None].astype(dtype)).reshape(b, nc, CHUNK, SSD_GROUPS, SSD_HPG, SSD_HEAD_DIM)
    Bc = Bm.reshape(b, nc, CHUNK, SSD_GROUPS, SSD_STATE)
    Cc = Cm.reshape(b, nc, CHUNK, SSD_GROUPS, SSD_STATE)
    a_cum = jnp.cumsum((dt * A).reshape(b, nc, CHUNK, SSD_GROUPS, SSD_HPG), axis=2)
    seg = a_cum[:, :, :, None] - a_cum[:, :, None, :]
    causal = jnp.tril(jnp.ones((CHUNK, CHUNK), dtype=bool))[None, None, :, :, None, None]
    Lmat = jnp.exp(jnp.where(causal, seg, -jnp.inf)).astype(dtype)
    cb = jnp.einsum('bclgn,bcsgn->bclsg', Cc, Bc)
    y_diag = jnp.einsum('bclsg,bclsgr,bcsgrp->bclgrp', cb, Lmat, xdt)
    decay_states = jnp.exp(a_cum[:, :, -1:] - a_cum).astype(dtype)
    states = jnp.einsum('bclgn,bclgr,bclgrp->bcgrpn', Bc, decay_states, xdt)
    chunk_decay = jnp.exp(a_cum[:, :, -1]).astype(dtype)

    def step(h, inp):
        s_c, d_c = inp
        return d_c[..., None, None] * h + s_c, h

    h0 = jnp.zeros_like(states[:, 0])
    _, prev = lax.scan(step, h0, (jnp.moveaxis(states, 1, 0), jnp.moveaxis(chunk_decay, 1, 0)))
    prev = jnp.moveaxis(prev, 0, 1)
    y_off = jnp.einsum('bclgn,bcgrpn,bclgr->bclgrp', Cc, prev, jnp.exp(a_cum).astype(dtype))
    return (y_diag + y_off).reshape(b, S, SSD_GROUPS, SSD_HPG, SSD_HEAD_DIM)

def mla_causal_attention(q_nope, q_rope, k_nope, k_rope, v):
    b, S = q_nope.shape[0], q_nope.shape[1]
    nblk = S // Q_BLOCK
    scale = 1.0 / math.sqrt(QK_DIM)
    qn_b = q_nope.reshape(b, nblk, Q_BLOCK, MLA_HEADS, QK_NOPE).swapaxes(0, 1)
    qr_b = q_rope.reshape(b, nblk, Q_BLOCK, MLA_HEADS, QK_ROPE).swapaxes(0, 1)
    starts = jnp.arange(nblk, dtype=jnp.int32) * Q_BLOCK
    k_idx = jnp.arange(S, dtype=jnp.int32)

    def one_block(args):
        qn, qr, start = args
        s = (jnp.einsum('bqhd,bkhd->bhqk', qn, k_nope)
             + jnp.einsum('bqhr,bkr->bhqk', qr, k_rope)).astype(jnp.float32) * scale
        q_idx = start + jnp.arange(Q_BLOCK, dtype=jnp.int32)
        mask = k_idx[None, :] <= q_idx[:, None]
        s = jnp.where(mask[None, None], s, -jnp.inf)
        p = jax.nn.softmax(s, axis=-1).astype(v.dtype)
        return jnp.einsum('bhqk,bkhv->bqhv', p, v)

    out = lax.map(one_block, (qn_b, qr_b, starts))
    return out.swapaxes(0, 1).reshape(b, S, MLA_HEADS * V_HEAD)

def hybrid_mixer(h, positions, w_in, conv_w, conv_b, dt_bias, a_log, d_skip, ssd_norm_w,
                 q_norm_w, w_uq, kv_norm_w, w_ukv, mla_norm_w, w_out):
    b, S = h.shape[0], h.shape[1]
    proj = h @ w_in
    z, xs, Bm, Cm, dt_raw, cq, ckv, k_rope_raw = jnp.split(proj, IN_SPLITS, axis=-1)

    xBC = jax.nn.silu(causal_depthwise_conv(jnp.concatenate([xs, Bm, Cm], axis=-1), conv_w, conv_b))
    xs, Bm, Cm = jnp.split(xBC, [D_SSD, D_SSD + SSD_GROUPS * SSD_STATE], axis=-1)
    dt = jax.nn.softplus(dt_raw.astype(jnp.float32) + dt_bias.astype(jnp.float32))
    A = -jnp.exp(a_log.astype(jnp.float32))
    xh = xs.reshape(b, S, SSD_GROUPS, SSD_HPG, SSD_HEAD_DIM)
    y = ssd_chunked(xh, dt.reshape(b, S, SSD_GROUPS, SSD_HPG), A.reshape(SSD_GROUPS, SSD_HPG),
                    Bm.reshape(b, S, SSD_GROUPS, SSD_STATE), Cm.reshape(b, S, SSD_GROUPS, SSD_STATE))
    y = y + d_skip.reshape(SSD_GROUPS, SSD_HPG)[:, :, None].astype(y.dtype) * xh
    yg = (y.reshape(b, S, D_SSD) * jax.nn.silu(z)).reshape(b, S, SSD_GROUPS, D_SSD // SSD_GROUPS)
    y_ssd = rmsnorm_2(yg, ssd_norm_w.reshape(SSD_GROUPS, D_SSD // SSD_GROUPS)).reshape(b, S, D_SSD)

    q = (rmsnorm_2(cq, q_norm_w) @ w_uq).reshape(b, S, MLA_HEADS, QK_DIM)
    q_nope, q_rope = jnp.split(q, [QK_NOPE], axis=-1)
    kv = (rmsnorm_2(ckv, kv_norm_w) @ w_ukv).reshape(b, S, MLA_HEADS, QK_NOPE + V_HEAD)
    k_nope, v = jnp.split(kv, [QK_NOPE], axis=-1)
    inv_freq = ROPE_THETA ** (-jnp.arange(0, QK_ROPE, 2, dtype=jnp.float32) / QK_ROPE)
    ang = positions[..., None].astype(jnp.float32) * inv_freq
    cos, sin = jnp.cos(ang).astype(h.dtype), jnp.sin(ang).astype(h.dtype)
    q_rope = apply_rope_2(q_rope, cos[:, :, None], sin[:, :, None])
    k_rope = apply_rope_2(k_rope_raw, cos, sin)
    attn = mla_causal_attention(q_nope, q_rope, k_nope, k_rope, v)
    y_mla = rmsnorm_2(attn, mla_norm_w)

    return jnp.concatenate([y_ssd, y_mla], axis=-1) @ w_out

def second_inputs(seed: int = 0) -> dict:
    key = jax.random.key(seed)
    ks = iter(jax.random.split(key, 40))

    def dense(shape, fan_in):
        return jax.random.normal(next(ks), shape, jnp.float32) * fan_in ** -0.5

    def gain(shape):
        return 1.0 + 0.05 * jax.random.normal(next(ks), shape, jnp.float32)

    def small(shape, s=0.02):
        return s * jax.random.normal(next(ks), shape, jnp.float32)

    L = DEPTH
    x = jax.random.normal(next(ks), (BATCH, SEQ, D_MODEL), jnp.float32)
    c = jax.random.normal(next(ks), (BATCH, D_MODEL), jnp.float32)
    offsets = jax.random.randint(next(ks), (BATCH, 1), 0, 1024, dtype=jnp.int32)
    positions = offsets + jnp.arange(SEQ, dtype=jnp.int32)[None, :]
    dt0 = jnp.exp(jax.random.uniform(next(ks), (L, SSD_HEADS), jnp.float32,
                                     math.log(1e-3), math.log(1e-1)))
    dt_bias = dt0 + jnp.log(-jnp.expm1(-dt0))
    a_log = jnp.log(jax.random.uniform(next(ks), (L, SSD_HEADS), jnp.float32, 1.0, 16.0))
    return {
        "x": x,
        "c": c,
        "positions": positions,
        "w_ada": dense((L, D_MODEL, N_MOD * D_MODEL), D_MODEL),
        "b_ada": small((L, N_MOD * D_MODEL)),
        "norm_ffn1": gain((L, D_MODEL)),
        "ffn1_w_gate": dense((L, D_MODEL, D_FF), D_MODEL),
        "ffn1_w_up": dense((L, D_MODEL, D_FF), D_MODEL),
        "ffn1_w_down": dense((L, D_FF, D_MODEL), D_FF),
        "norm_mix": gain((L, D_MODEL)),
        "w_in": dense((L, D_MODEL, D_IN_PROJ), D_MODEL),
        "conv_w": dense((L, CONV_WIDTH, D_CONV), CONV_WIDTH),
        "conv_b": small((L, D_CONV)),
        "dt_bias": dt_bias,
        "a_log": a_log,
        "d_skip": gain((L, SSD_HEADS)),
        "ssd_norm_w": gain((L, D_SSD)),
        "q_norm_w": gain((L, Q_LORA)),
        "w_uq": dense((L, Q_LORA, MLA_HEADS * QK_DIM), Q_LORA),
        "kv_norm_w": gain((L, KV_LORA)),
        "w_ukv": dense((L, KV_LORA, MLA_HEADS * (QK_NOPE + V_HEAD)), KV_LORA),
        "mla_norm_w": gain((L, D_MLA)),
        "w_out": dense((L, D_MIX, D_MODEL), D_MIX),
        "norm_ffn2": gain((L, D_MODEL)),
        "ffn2_w_gate": dense((L, D_MODEL, D_FF), D_MODEL),
        "ffn2_w_up": dense((L, D_MODEL, D_FF), D_MODEL),
        "ffn2_w_down": dense((L, D_FF, D_MODEL), D_FF),
        "norm_final": gain((D_MODEL,)),
    }

def second_block(x, c, positions, w_ada, b_ada, norm_ffn1, ffn1_w_gate, ffn1_w_up, ffn1_w_down,
              norm_mix, w_in, conv_w, conv_b, dt_bias, a_log, d_skip, ssd_norm_w,
              q_norm_w, w_uq, kv_norm_w, w_ukv, mla_norm_w, w_out,
              norm_ffn2, ffn2_w_gate, ffn2_w_up, ffn2_w_down, norm_final):
    c_act = jax.nn.silu(c)
    for l in range(DEPTH):
        mod = c_act @ w_ada[l] + b_ada[l]
        (sh1, sc1, g1, sh2, sc2, g2, sh3, sc3, g3) = jnp.split(mod, N_MOD, axis=-1)
        h = modulate(rmsnorm_2(x, norm_ffn1[l]), sh1, sc1)
        x = x + 0.5 * g1[:, None, :] * swiglu(h, ffn1_w_gate[l], ffn1_w_up[l], ffn1_w_down[l])
        h = modulate(rmsnorm_2(x, norm_mix[l]), sh2, sc2)
        x = x + g2[:, None, :] * hybrid_mixer(
            h, positions, w_in[l], conv_w[l], conv_b[l], dt_bias[l], a_log[l], d_skip[l],
            ssd_norm_w[l], q_norm_w[l], w_uq[l], kv_norm_w[l], w_ukv[l], mla_norm_w[l], w_out[l])
        h = modulate(rmsnorm_2(x, norm_ffn2[l]), sh3, sc3)
        x = x + 0.5 * g3[:, None, :] * swiglu(h, ffn2_w_gate[l], ffn2_w_up[l], ffn2_w_down[l])
    return rmsnorm_2(x, norm_final)


def setup_inputs(seed=0):
    out = dict(first_inputs(seed))
    for name, value in second_inputs(seed + 1).items():
        if name != "x":
            out[name + "_2"] = value
    return out


def reference(
    x, meta_tokens, mix_norm_w, w_in, rec_lb_logits, rec_norm_w, diff_lambda_q1, diff_lambda_k1,
    diff_lambda_q2, diff_lambda_k2, diff_subln_w, w_out, ffn_norm_w, peer_w_query, peer_subkeys,
    peer_u, peer_v, final_norm_w, c_2, positions_2, w_ada_2, b_ada_2, norm_ffn1_2,
    ffn1_w_gate_2, ffn1_w_up_2, ffn1_w_down_2, norm_mix_2, w_in_2, conv_w_2, conv_b_2,
    dt_bias_2, a_log_2, d_skip_2, ssd_norm_w_2, q_norm_w_2, w_uq_2, kv_norm_w_2, w_ukv_2,
    mla_norm_w_2, w_out_2, norm_ffn2_2, ffn2_w_gate_2, ffn2_w_up_2, ffn2_w_down_2, norm_final_2,
):
    x = first_block(
        x, meta_tokens, mix_norm_w, w_in, rec_lb_logits, rec_norm_w, diff_lambda_q1,
        diff_lambda_k1, diff_lambda_q2, diff_lambda_k2, diff_subln_w, w_out, ffn_norm_w,
        peer_w_query, peer_subkeys, peer_u, peer_v, final_norm_w,
    )
    return second_block(
        x, c_2, positions_2, w_ada_2, b_ada_2, norm_ffn1_2, ffn1_w_gate_2, ffn1_w_up_2,
        ffn1_w_down_2, norm_mix_2, w_in_2, conv_w_2, conv_b_2, dt_bias_2, a_log_2, d_skip_2,
        ssd_norm_w_2, q_norm_w_2, w_uq_2, kv_norm_w_2, w_ukv_2, mla_norm_w_2, w_out_2,
        norm_ffn2_2, ffn2_w_gate_2, ffn2_w_up_2, ffn2_w_down_2, norm_final_2,
    )


_drawn_inputs = setup_inputs


def setup_inputs(seed=0):
    import zlib

    import numpy as np

    out = dict(_drawn_inputs(seed))
    spreads = {}
    factors = {'rec_norm_w': 3.631,
     'diff_lambda_k2': 6.195,
     'diff_subln_w': 2.832,
     'final_norm_w': 2.75,
     'norm_ffn1_2': 2.745,
     'conv_b_2': 7.426,
     'd_skip_2': 28.158,
     'ssd_norm_w_2': 9.423,
     'q_norm_w_2': 8.0,
     'kv_norm_w_2': 3.312,
     'mla_norm_w_2': 9.015,
     'norm_ffn2_2': 3.38}
    for name, (base, spread) in spreads.items():
        noise = np.random.default_rng([zlib.crc32(name.encode()), seed]).standard_normal(out[name].shape)
        drawn = base * np.exp(spread * noise) if base else spread * noise
        out[name] = __import__('jax').numpy.asarray(drawn.astype(out[name].dtype))
    for name, factor in factors.items():
        out[name] = (out[name] * factor).astype(out[name].dtype)
    return out
```

```python
import math
from contextlib import ExitStack

import concourse.bass as bass
import numpy as np
from concourse import mybir

F32 = mybir.dt.float32
F32R = mybir.dt.float32r
U32 = mybir.dt.uint32
I32 = mybir.dt.int32
ALU = mybir.AluOpType
ACT = mybir.ActivationFunctionType
AX = mybir.AxisListType

P = 128
D = 1024
KC = D // P
T = 512
TT = T // P
NM = 16
NT = NM + T
HALF = NT // 2
BANK = 512
EPS = 1e-6
NEG = -3.0e38
LOWEST = -3.4e38

AH, AHD, AV = 4, 64, 128
RH, RK = 4, 128
SUB = 16
NCH = NT // SUB
LAM0 = 0.2
PH, TOPK, NK = 8, 16, 128
SLOTS = PH * TOPK

FF = 2816
FB = FF // P
SH, SHD, SG, SN = 16, 64, 2, 128
HPG = SH // SG
MH, NOPE, ROPE, MV = 8, 64, 32, 128
QKD = NOPE + ROPE
QL, KVL = 384, 256


class Chain:

    def __init__(self, engine, semaphore, start):
        self.engine, self.semaphore, self.count, self.base = engine, semaphore, start, 0

    def link(self, instruction):
        self.count += 1
        instruction.then_inc(self.semaphore, 1)
        self.engine.wait_ge(self.semaphore, self.base + self.count)


class Core:

    def __init__(self, nc, ctx):
        self.nc, self.ctx, self.steps, self.sems = nc, ctx, {}, {}

    def sem(self, name):
        if name not in self.sems:
            self.sems[name] = [self.nc.alloc_semaphore(name=numbered(name)), 0]
        return self.sems[name][0]

    def start_over(self):
        self.nc.clear_and_free_semaphores([handle for handle, _ in self.sems.values()])
        self.nc.all_engine_barrier()
        self.sems, self.steps = {}, {}

    def chain(self, engine, name):
        if name not in self.steps:
            self.steps[name] = Chain(engine, self.sem(name), 0)
        self.steps[name].engine = engine
        return self.steps[name]


class Signal:

    def __init__(self, core, name):
        self.core, self.name, self.handle = core, name, core.sem(name)
        self.base = core.sems[name][1]

    def at(self, n):
        return self.base + n

    def used(self, n):
        self.core.sems[self.name][1] = self.base + n


NAMES = {}


def numbered(name):
    NAMES[name] = NAMES.get(name, 0) + 1
    return name if NAMES[name] == 1 else f"{name}_{NAMES[name]}"


def sbuf(nc, ctx, name, shape, dtype=F32):
    return ctx.enter_context(nc.sbuf_tensor(numbered(name), shape, dtype))


def psum(nc, ctx, name, shape):
    return ctx.enter_context(nc.psum_tensor(numbered(name), shape, F32))


class Parts:

    def __init__(self, core, ctx, name, shape):
        self.high = sbuf(core.nc, ctx, f"{name}_high", shape, F32R)
        self.low = sbuf(core.nc, ctx, f"{name}_low", shape, F32R)


def product(pe, out, left, right, start, stop):
    pe.matmul(out, left[0], right[0], start=start, stop=False)
    pe.matmul(out, left[0], right[1], start=False, stop=False)
    return pe.matmul(out, left[1], right[0], start=False, stop=stop)


def norm_to_features(core, x, ident, feat, scale, bias=None, meta=None):
    nc = core.nc
    first = NM if meta is not None else 0
    with ExitStack() as ctx:
        xn = sbuf(nc, ctx, "norm_x", [P, TT, D])
        sq = sbuf(nc, ctx, "norm_sq", [P, D])
        ss = sbuf(nc, ctx, "norm_ss", [P, TT + 1])
        rstd = sbuf(nc, ctx, "norm_rstd", [P, TT + 1])
        full = sbuf(nc, ctx, "norm_full", [P, 4, T])
        xm = sbuf(nc, ctx, "norm_xm", [NM, D]) if meta is not None else None
        banks = [psum(nc, ctx, f"norm_bank{i}", [P, BANK]) for i in range(7)]
        mbank = psum(nc, ctx, "norm_meta", [P, KC * NM])
        ss_clear, sq_done, ms_ready, rstd_ready, xn_ready, turned, whole, high, low = [
            Signal(core, f"norm_{n}") for n in ("ss_clear", "sq_done", "ms_ready", "rstd_ready", "xn_ready",
                                                "turned", "whole", "high", "low")]
        tiles = [(x[:, t, :], xn[:, t, :], P) for t in range(TT)]
        if meta is not None:
            tiles.append((meta, xm[:, :], NM))
        n_tiles = len(tiles)
        block = ctx.enter_context(nc.Block())

        @block.scalar
        def _(act):
            act.wait_ge(ss_clear.handle, ss_clear.at(1))
            for t, (src, _, rows) in enumerate(tiles):
                if t:
                    act.wait_ge(sq_done.handle, sq_done.at(t))
                act.activation(sq[0:rows, :], src, ACT.Square, accum_out=ss[0:rows, t:t + 1])\
                   .then_inc(sq_done.handle, 1)
            act.wait_ge(ms_ready.handle, ms_ready.at(1))
            act.activation(rstd[:, 0:n_tiles], rstd[:, 0:n_tiles], ACT.Sqrt).then_inc(rstd_ready.handle, 1)
            for f in range(KC):
                act.wait_ge(whole.handle, whole.at(f + 1))
                act.activation(feat.high[:, f, first:first + T], full[:, f % 4, :], ACT.Copy).then_inc(high.handle, 1)

        @block.vector
        def _(dve):
            chain = core.chain(dve, "dve_step")
            dve.memset(ss[:, :], float(D)).then_inc(ss_clear.handle, 1)
            dve.wait_ge(sq_done.handle, sq_done.at(n_tiles))
            chain.link(dve.tensor_scalar(rstd[:, 0:n_tiles], ss[:, 0:n_tiles], 1.0 / D, EPS, ALU.mult, ALU.add))
            dve.reciprocal(rstd[:, 0:n_tiles], rstd[:, 0:n_tiles]).then_inc(ms_ready.handle, 1)
            dve.wait_ge(rstd_ready.handle, rstd_ready.at(1))
            for t, (src, dst, rows) in enumerate(tiles):
                dve.tensor_scalar(dst, src, rstd[0:rows, t:t + 1], None, ALU.mult).then_inc(xn_ready.handle, 1)
            for f in range(KC + 1):
                if f < KC:
                    dve.wait_ge(turned.handle, turned.at(f + 1))
                    if f >= 4:
                        dve.wait_ge(low.handle, low.at(f - 3))
                    if bias is not None:
                        dve.tensor_scalar(full[:, f % 4, :], banks[f % 7][:, :], scale[:, f:f + 1], bias[:, f:f + 1],
                                          ALU.mult, ALU.add).then_inc(whole.handle, 1)
                    else:
                        dve.tensor_scalar(full[:, f % 4, :], banks[f % 7][:, :], scale[:, f:f + 1], None, ALU.mult)\
                           .then_inc(whole.handle, 1)
                if f >= 1:
                    dve.wait_ge(high.handle, high.at(f))
                    dve.tensor_tensor(feat.low[:, f - 1, first:first + T], full[:, (f - 1) % 4, :],
                                      feat.high[:, f - 1, first:first + T].bitcast(F32), ALU.subtract)\
                       .then_inc(low.handle, 1)
            if meta is not None:
                dve.wait_ge(turned.handle, turned.at(KC + 1))
                dve.wait_ge(low.handle, low.at(KC))
                mfull = full[:, 0, 0:KC * NM].rearrange("p (f t) -> p f t", t=NM)
                chain.link(dve.tensor_tensor(mfull, mbank[:, :].rearrange("p (f t) -> p f t", t=NM),
                                             scale[:, :].unsqueeze(2).broadcast_to([P, KC, NM]), ALU.mult))
                chain.link(dve.tensor_copy(feat.high[:, :, 0:NM], mfull))
                chain.link(dve.tensor_tensor(feat.low[:, :, 0:NM], mfull, feat.high[:, :, 0:NM].bitcast(F32), ALU.subtract))

        @block.tensor
        def _(pe):
            pe.wait_ge(xn_ready.handle, xn_ready.at(n_tiles))
            for f in range(KC):
                if f == 7:
                    pe.wait_ge(whole.handle, whole.at(1))
                for t in range(TT):
                    last = pe.transpose(banks[f % 7][:, t * P:(t + 1) * P], xn[:, t, f * P:(f + 1) * P], ident[:, :])
                last.then_inc(turned.handle, 1)
            if meta is not None:
                for f in range(KC):
                    last = pe.transpose(mbank[:, f * NM:(f + 1) * NM], xm[:, f * P:(f + 1) * P], ident[0:NM, 0:NM])
                last.then_inc(turned.handle, 1)

        for s, n in ((ss_clear, 1), (sq_done, n_tiles), (ms_ready, 1), (rstd_ready, 1), (xn_ready, n_tiles),
                     (turned, KC + (meta is not None)), (whole, KC), (high, KC), (low, KC)):
            s.used(n)


def load_first(core, t, dram):
    nc = core.nc
    with ExitStack() as ctx:
        loaded = core.sem("loaded")
        lb_in = sbuf(nc, ctx, "lb_in", [P, 2, RH])
        lb_top = sbuf(nc, ctx, "lb_top", [P, RH])
        lam_in = sbuf(nc, ctx, "lam_in", [P, 4, AHD])
        lam_junk = sbuf(nc, ctx, "lam_junk", [P, 2, AHD])
        lam_e = sbuf(nc, ctx, "lam_e", [P, 2])
        dots, exps = core.sem("small_dots"), core.sem("small_exps")
        block = ctx.enter_context(nc.Block())
        n_loads = 11
        c_in = core.sem("c_in")

        @block.sync
        def _(sp):
            sp.dma_start(t.c_col[:, :], dram["c_2"]).then_inc(c_in, 16)
            sp.dma_start(t.meta[:, :], dram["meta_tokens"]).then_inc(loaded, 16)
            sp.dma_start(t.x[:, :, :], dram["x"].rearrange("o (t p) d -> p (o t) d", p=P)).then_inc(loaded, 16)
            sp.dma_start(t.ident[:, :], dram["ident"]).then_inc(loaded, 16)
            sp.dma_start(t.mix_norm[:, :], dram["mix_norm_w"]).then_inc(loaded, 16)
            sp.dma_start(lb_in[:, :, :], dram["rec_lb_logits"]).then_inc(loaded, 16)
            for n, name in enumerate(("diff_lambda_q1", "diff_lambda_k1", "diff_lambda_q2", "diff_lambda_k2")):
                sp.dma_start(lam_in[:, n, :], dram[name].broadcast_to([P, AHD])).then_inc(loaded, 16)
            sp.dma_start(t.mixed_scale[:, 0:AH], dram["diff_subln_w"]).then_inc(loaded, 16)
            sp.dma_start(t.mixed_scale[:, AH:AH + RH], dram["rec_norm_w"]).then_inc(loaded, 16)

        @block.vector
        def _(dve):
            chain = core.chain(dve, "dve_step")
            dve.wait_ge(loaded, 16 * n_loads)
            for n in range(2):
                last = dve.tensor_tensor_reduce(out=lam_junk[:, n, :], in0=lam_in[:, 2 * n, :], in1=lam_in[:, 2 * n + 1, :],
                                                scale=1.0, scalar=0.0, op0=ALU.mult, op1=ALU.add,
                                                accum_out=lam_e[:, n:n + 1])
                chain.link(last)
            chain.link(dve.tensor_tensor(lb_top[:, :], lb_in[:, 0, :], lb_in[:, 1, :], ALU.max))
            dve.tensor_tensor(lb_in[:, :, :], lb_in[:, :, :], lb_top[:, :].unsqueeze(1).broadcast_to([P, 2, RH]),
                              ALU.subtract).then_inc(dots, 1)
            chain.link(dve.tensor_scalar(t.mixed_scale[:, 0:AH], t.mixed_scale[:, 0:AH], 1.0 - LAM0, None, ALU.mult))
            dve.wait_ge(exps, 2)
            chain.link(dve.tensor_tensor(t.neg_lam[:, :], lam_e[:, 1:2], lam_e[:, 0:1], ALU.subtract))
            chain.link(dve.tensor_scalar(t.neg_lam[:, :], t.neg_lam[:, :], -LAM0, None, ALU.add))
            chain.link(dve.tensor_tensor(lb_top[:, :], lb_in[:, 0, :], lb_in[:, 1, :], ALU.add))
            chain.link(dve.reciprocal(lb_top[:, :], lb_top[:, :]))
            chain.link(dve.tensor_tensor(t.lb[:, :], lb_in[:, 0, :], lb_top[:, :], ALU.mult))
            chain.link(dve.tensor_scalar(t.one_lb[:, :], t.lb[:, :], -1.0, 1.0, ALU.mult, ALU.add))

        @block.scalar
        def _(act):
            act.wait_ge(c_in, 16)
            act.activation(t.c_col[:, :], t.c_col[:, :], ACT.Silu)
            act.wait_ge(dots, 1)
            act.activation(lam_e[:, :], lam_e[:, :], ACT.Exp).then_inc(exps, 1)
            act.activation(lb_in[:, :, :], lb_in[:, :, :], ACT.Exp).then_inc(exps, 1)


class Slab:

    def __init__(self, source, wide, ranges, outs, k0=0, width=P):
        self.source, self.wide, self.ranges, self.outs = source, wide, ranges, outs
        self.k0, self.width = k0, width


def feature_slab(source, b, ranges, first):
    return Slab(source[b], False, ranges, list(range(first, first + len(ranges))))


def token_slabs(source, ranges, first, width=BANK):
    return [Slab(source[:, k:k + 2, :], True, ranges, list(range(first, first + len(ranges))), k, width)
            for k in range(0, KC, 2)]


def project(core, feat, slabs, moves, beside=None, beside_dve=None, before_moves=None, beside_act=None):
    nc = core.nc
    RAW, RING, BANKS = 3, 2, 8
    N = len(slabs)
    with ExitStack() as ctx:
        w_raw = sbuf(nc, ctx, "proj_raw", [P, RAW, D])
        w = Parts(core, ctx, "proj_w", [P, RING, D])
        banks = [psum(nc, ctx, f"proj_bank{i}", [P, BANK]) for i in range(BANKS)]
        w_in = [Signal(core, f"proj_in{i}") for i in range(RAW)]
        high, low, used, out_done, moved = [Signal(core, f"proj_{n}") for n in ("high", "low", "used", "out_done", "moved")]
        block = ctx.enter_context(nc.Block())

        def taken(slab):
            return KC * P if not slab.wide else 2 * slab.width

        def view(ring, slot, slab):
            ap = ring[:, slot, 0:taken(slab)]
            return ap.rearrange("p (k n) -> p k n", k=2 if slab.wide else KC)

        @block.sync
        def _(sp):
            for n, slab in enumerate(slabs):
                if n >= RAW:
                    sp.wait_ge(low.handle, low.at(n - RAW + 1))
                dst = view(w_raw, n % RAW, slab) if slab.wide else w_raw[:, n % RAW, :]
                sp.dma_start(dst, slab.source).then_inc(w_in[n % RAW].handle, 16)

        @block.tensor
        def _(pe):
            for n, slab in enumerate(slabs):
                pe.wait_ge(low.handle, low.at(n + 1))
                hi, lo = view(w.high, n % RING, slab), view(w.low, n % RING, slab)
                for (at, count), e in zip(slab.ranges, slab.outs):
                    opens = not slab.wide or slab.k0 == 0
                    closes = not slab.wide or slab.k0 == KC - 2
                    if opens and e >= BANKS:
                        pe.wait_ge(moved.handle, moved.at(e - BANKS + 1))
                    chunks = range(KC) if not slab.wide else range(2)
                    for k in chunks:
                        tokens = slice(at, at + count)
                        start, stop = opens and k == 0, closes and k == chunks[-1]
                        act = (feat.high[:, slab.k0 + k, tokens], feat.low[:, slab.k0 + k, tokens])
                        if slab.wide:
                            last = product(pe, banks[e % BANKS][:, 0:slab.width], act, (hi[:, k, :], lo[:, k, :]),
                                           start, stop)
                        else:
                            last = product(pe, banks[e % BANKS][:, 0:count], (hi[:, k, :], lo[:, k, :]), act, start, stop)
                    if e == slab.outs[-1]:
                        last.then_inc(used.handle, 1)
                    elif closes:
                        last.then_inc(out_done.handle, 1)

        @block.scalar
        def _(act):
            def weights_high(n):
                slab, ring = slabs[n], w_in[n % RAW]
                act.wait_ge(ring.handle, ring.at(16 * (n // RAW + 1)))
                if n >= RING:
                    act.wait_ge(used.handle, used.at(n - RING + 1))
                act.activation(w.high[:, n % RING, 0:taken(slab)], w_raw[:, n % RAW, 0:taken(slab)], ACT.Copy)\
                   .then_inc(high.handle, 1)

            weights_high(0)
            weights_high(1)
            closed = 0
            for n, slab in enumerate(slabs):
                act.wait_ge(used.handle, used.at(n + 1))
                if n + 2 < N:
                    weights_high(n + 2)
                if before_moves is not None:
                    before_moves(act, n)
                for e in (slab.outs if not slab.wide or slab.k0 == KC - 2 else []):
                    if e != slab.outs[-1]:
                        closed += 1
                        act.wait_ge(out_done.handle, out_done.at(closed))
                    for i, (dst, rows, cols) in enumerate(moves[e]):
                        last = act.activation(dst, banks[e % BANKS][rows, cols], ACT.Copy)
                    last.then_inc(moved.handle, 1)
                if beside_act is not None:
                    beside_act(act, n)
            out_done.total = closed

        @block.vector
        def _(dve):
            for n, slab in enumerate(slabs):
                dve.wait_ge(high.handle, high.at(n + 1))
                dve.tensor_tensor(w.low[:, n % RING, 0:taken(slab)], w_raw[:, n % RAW, 0:taken(slab)],
                                  w.high[:, n % RING, 0:taken(slab)].bitcast(F32), ALU.subtract).then_inc(low.handle, 1)
                if beside_dve is not None:
                    beside_dve(dve, n, moved)

        if beside is not None:
            beside(block)
        for i, ring in enumerate(w_in):
            ring.used(16 * len(range(i, N, RAW)))
        for s, n in ((high, N), (low, N), (used, N), (out_done, out_done.total), (moved, len(moves))):
            s.used(n)


def first_projection(core, t, dram, feat):
    FBL, ACH = 16, 1536
    PARTS, PER_SLAB = 9 * D // ACH, 2
    halves = [(0, HALF), (HALF, HALF)]
    tiles = [(NM + tile * P, P) for tile in range(TT)]
    slabs, moves = [], []
    for b in range(FBL):
        slabs.append(feature_slab(dram["w_in_f"], b, halves, len(moves)))
        moves += [[(t.fm[:, b, at:at + n], slice(0, P), slice(0, n))] for at, n in halves]
    for c in range(3):
        ranges = tiles + ([(0, P)] if c < 2 else [])
        slabs += token_slabs(dram["w_in_t"][c], ranges, len(moves))
        moves += [[(t.tm[:, c, tile, :], slice(0, P), slice(0, BANK))] for tile in range(TT)]
        if c < 2:
            moves.append([(t.tm_meta[:, c, :], slice(0, NM), slice(0, BANK))])
    with ExitStack() as ctx:
        ada = sbuf(core.nc, ctx, "ada", [P, 2, ACH])
        ada_in = [core.sem(f"ada_in{i}") for i in range(2)]
        ada_used, acc_clear, acc_bias = core.sem("ada_used"), core.sem("acc_clear"), core.sem("acc_bias")
        N = PARTS * KC
        assert N <= PER_SLAB * len(slabs)

        def beside(block):
            @block.gpsimd
            def _(pool):
                pool.memset(t.ada_acc[:, :], 0.0).then_inc(acc_clear, 1)
                pool.wait_ge(acc_clear, 1)
                pool.dma_start(t.ada_acc[0:1, :], dram["b_ada_2"]).then_inc(acc_bias, 16)
                for n in range(N):
                    if n >= 2:
                        pool.wait_ge(ada_used, n - 1)
                    k, part = n // PARTS, n % PARTS
                    pool.dma_start(ada[:, n % 2, :], dram["w_ada_2"][0, k * P:(k + 1) * P, part * ACH:(part + 1) * ACH])\
                        .then_inc(ada_in[n % 2], 16)

        def beside_dve(dve, slab, moved):
            for n in range(PER_SLAB * slab, min(N, PER_SLAB * (slab + 1))):
                if n == 0:
                    dve.wait_ge(acc_bias, 16)
                k, part = n // PARTS, n % PARTS
                dve.wait_ge(ada_in[n % 2], 16 * (n // 2 + 1))
                if n >= PARTS:
                    dve.wait_ge(ada_used, n - PARTS + 1)
                acc = t.ada_acc[:, part * ACH:(part + 1) * ACH]
                dve.scalar_tensor_tensor(acc, ada[:, n % 2, :], t.c_col[:, k:k + 1], acc, ALU.mult, ALU.add)\
                   .then_inc(ada_used, 1)

        project(core, feat, slabs, moves, beside, beside_dve)


def rotate_first(core, t, dram):
    nc = core.nc
    with ExitStack() as ctx:
        turn = sbuf(nc, ctx, "turn", [P, P])
        cos = sbuf(nc, ctx, "cos", [P, NT])
        sin = sbuf(nc, ctx, "sin", [P, NT])
        swung = sbuf(nc, ctx, "swung", [P, 2, NT])
        bank = [psum(nc, ctx, f"rot_bank{i}", [P, 2, BANK]) for i in range(2)]
        tables, turned, swung_done, rotated = [core.sem(f"rope_{n}") for n in ("tables", "turned", "swung", "rotated")]
        block = ctx.enter_context(nc.Block())

        @block.sync
        def _(sp):
            sp.dma_start(turn[:, :], dram["rope_turn"]).then_inc(tables, 16)
            sp.dma_start(cos[:, :], dram["rope_cos"]).then_inc(tables, 16)
            sp.dma_start(sin[:, :], dram["rope_sin"]).then_inc(tables, 16)

        @block.tensor
        def _(pe):
            pe.wait_ge(tables, 48)
            for b in range(2 * AH):
                if b >= 2:
                    pe.wait_ge(swung_done, b - 1)
                for half in range(2):
                    last = pe.matmul(bank[b % 2][:, half, 0:HALF], turn[:, :], t.fm[:, b, half * HALF:(half + 1) * HALF],
                                     start=True, stop=True)
                last.then_inc(turned, 1)

        @block.vector
        def _(dve):
            chain = core.chain(dve, "dve_step")
            for b in range(2 * AH):
                dve.wait_ge(turned, b + 1)
                dve.tensor_tensor(swung[:, b % 2, :].rearrange("p (a n) -> p a n", a=2), bank[b % 2][:, :, 0:HALF],
                                  sin[:, :].rearrange("p (a n) -> p a n", a=2), ALU.mult).then_inc(swung_done, 1)
                chain.link(dve.tensor_tensor(t.fm[:, b, :], t.fm[:, b, :], cos[:, :], ALU.mult))
                dve.wait_ge(swung_done, b + 1)
                chain.link(dve.tensor_tensor(t.fm[:, b, :], t.fm[:, b, :], swung[:, b % 2, :], ALU.add))


def first_attention(core, t, dram):
    nc = core.nc
    scale = AHD ** -0.5
    units = [(h, i) for h in range(AH) for i in range(TT)]
    with ExitStack() as ctx:
        mask = sbuf(nc, ctx, "mask", [P, P])
        prob = sbuf(nc, ctx, "prob", [P, 2, 2, NT])
        weight = sbuf(nc, ctx, "weight", [P, 2, NT])
        w_turned = sbuf(nc, ctx, "w_turned", [P, 2, TT, P])
        w_meta = sbuf(nc, ctx, "w_meta", [NM, 2, P])
        stat = sbuf(nc, ctx, "stat", [P, 2, 2, 4])
        score = [psum(nc, ctx, f"score{i}", [P, 2 * BANK]) for i in range(2)]
        turn_bank = psum(nc, ctx, "turn_bank", [P, TT, P])
        meta_bank = psum(nc, ctx, "meta_bank", [NM, P])
        out_bank = [psum(nc, ctx, f"out_bank{i}", [P, P]) for i in range(2)]
        mask_in = core.sem("mask_in")
        scored, max_ready, exp_done, weighed, turned, turned_moved, summed, out_moved = [
            core.sem(f"att_{n}") for n in ("scored", "max", "exp", "weighed", "turned", "turned_moved", "summed", "out_moved")]
        block = ctx.enter_context(nc.Block())

        @block.sync
        def _(sp):
            sp.dma_start(mask[:, :], dram["causal"]).then_inc(mask_in, 16)

        @block.tensor
        def _(pe):
            def scores(u):
                h, i = units[u]
                for half in range(2):
                    if u >= 1:
                        pe.wait_ge(exp_done, 2 * (u - 1) + half + 1)
                    rows = slice(half * AHD, (half + 1) * AHD)
                    q = t.fm[rows, h, NM + i * P:NM + (i + 1) * P]
                    pe.matmul(score[half][:, BANK - NM:BANK], q, t.fm[rows, AH + h, 0:NM], start=True, stop=True)
                    pe.matmul(score[half][:, BANK:BANK + (i + 1) * P], q, t.fm[rows, AH + h, NM:NM + (i + 1) * P],
                              start=True, stop=True).then_inc(scored, 1)

            def turn(u):
                h, i = units[u]
                pe.wait_ge(weighed, u + 1)
                if u >= 1:
                    pe.wait_ge(turned_moved, 2 * u)
                pe.transpose(meta_bank[:, :], weight[:, u % 2, 0:NM], t.ident[:, :])
                for j in range(i + 1):
                    last = pe.transpose(turn_bank[:, j, :], weight[:, u % 2, NM + j * P:NM + (j + 1) * P], t.ident[:, :])
                last.then_inc(turned, 1)

            def sums(u):
                h, i = units[u]
                pe.wait_ge(turned_moved, 2 * u + 2)
                if u >= 2:
                    pe.wait_ge(out_moved, u - 1)
                v = slice(h * AV, (h + 1) * AV)
                pe.matmul(out_bank[u % 2][:, :], w_meta[:, u % 2, :], t.tm_meta[:, 0, v], start=True, stop=False)
                for j in range(i + 1):
                    last = pe.matmul(out_bank[u % 2][:, :], w_turned[:, u % 2, j, :], t.tm[:, 0, j, v],
                                     start=False, stop=(j == i))
                last.then_inc(summed, 1)

            scores(0)
            for u in range(len(units)):
                if u + 1 < len(units):
                    scores(u + 1)
                if u >= 1:
                    sums(u - 1)
                turn(u)
            sums(len(units) - 1)

        def move_turned(act, u):
            i = units[u][1]
            act.wait_ge(turned, u + 1)
            if u >= 2:
                act.wait_ge(summed, u - 1)
            act.activation(w_meta[:, u % 2, :], meta_bank[:, :], ACT.Copy).then_inc(turned_moved, 1)
            act.activation(w_turned[:, u % 2, 0:i + 1, :], turn_bank[:, 0:i + 1, :], ACT.Copy).then_inc(turned_moved, 1)

        @block.scalar
        def _(act):
            for u, (h, i) in enumerate(units):
                n = NM + (i + 1) * P
                for half in range(2):
                    act.wait_ge(max_ready, 2 * u + half + 1)
                    if u >= 2:
                        act.wait_ge(weighed, u - 1)
                    act.activation(prob[:, u % 2, half, 0:n], score[half][:, BANK - NM:BANK - NM + n], ACT.Exp,
                                   bias=stat[:, u % 2, half, 1:2], scale=scale,
                                   accum_out=stat[:, u % 2, half, 2:3]).then_inc(exp_done, 1)
                if u >= 1:
                    move_turned(act, u - 1)
            move_turned(act, len(units) - 1)

        @block.vector
        def _(dve):
            chain = core.chain(dve, "dve_step")
            dve.wait_ge(mask_in, 16)

            def maxima(u):
                h, i = units[u]
                n = NM + (i + 1) * P
                for half in range(2):
                    dve.wait_ge(scored, 2 * u + half + 1)
                    diag = score[half][:, BANK + i * P:BANK + (i + 1) * P]
                    chain.link(dve.tensor_tensor(diag, diag, mask[:, :], ALU.add))
                    chain.link(dve.reduce_max(stat[:, u % 2, half, 0:1], score[half][:, BANK - NM:BANK - NM + n], AX.X))
                    dve.tensor_scalar(stat[:, u % 2, half, 1:2], stat[:, u % 2, half, 0:1], -scale, None, ALU.mult)\
                       .then_inc(max_ready, 1)

            def weights(u):
                h, i = units[u]
                n = NM + (i + 1) * P
                dve.wait_ge(exp_done, 2 * u + 2)
                for half in range(2):
                    chain.link(dve.reciprocal(stat[:, u % 2, half, 3:4], stat[:, u % 2, half, 2:3]))
                chain.link(dve.tensor_tensor(stat[:, u % 2, 1, 3:4], stat[:, u % 2, 1, 3:4], t.neg_lam[:, :], ALU.mult))
                if u >= 2:
                    dve.wait_ge(turned, u - 1)
                chain.link(dve.tensor_scalar(weight[:, u % 2, 0:n], prob[:, u % 2, 0, 0:n], stat[:, u % 2, 0, 3:4],
                                             None, ALU.mult))
                dve.scalar_tensor_tensor(weight[:, u % 2, 0:n], prob[:, u % 2, 1, 0:n], stat[:, u % 2, 1, 3:4],
                                         weight[:, u % 2, 0:n], ALU.mult, ALU.add).then_inc(weighed, 1)

            def outputs(u):
                h, i = units[u]
                dve.wait_ge(summed, u + 1)
                dve.tensor_copy(t.mixed[:, i, h * AV:(h + 1) * AV], out_bank[u % 2][:, :]).then_inc(out_moved, 1)

            maxima(0)
            for u in range(len(units)):
                if u + 1 < len(units):
                    maxima(u + 1)
                weights(u)
                if u >= 1:
                    outputs(u - 1)
            outputs(len(units) - 1)


def gla_prepare(core, t, dram):
    nc = core.nc
    Q, K = 2 * AH, 2 * AH + RH
    RING = 3
    with ExitStack() as ctx:
        cum = sbuf(nc, ctx, "cum", [P, RH, NT])
        keep = sbuf(nc, ctx, "keep", [P, NT])
        one_hot = sbuf(nc, ctx, "one_hot", [P, SUB, SUB])
        pair = sbuf(nc, ctx, "pair", [P, RING, RH, NCH - 1, SUB])
        a_bank = [psum(nc, ctx, f"a_bank{h}", [SUB, (NCH - 1) * SUB]) for h in range(RH)]
        tables, gated, logs, cum_done, exps, decays, within = [
            core.sem(f"gla_{n}") for n in ("tables", "gated", "logs", "cum", "exps", "decays", "within")]
        sigmoids, pair_diff, pair_exp, pair_done, pair_used = [
            core.sem(f"gla_{n}") for n in ("sigmoids", "pair_diff", "pair_exp", "pair_done", "pair_used")]
        block = ctx.enter_context(nc.Block())
        q, k = t.fm[:, Q:Q + RH, :], t.fm[:, K:K + RH, :]

        def steps(ap):
            return ap.rearrange("p h (n s) -> p h n s", s=SUB)

        @block.sync
        def _(sp):
            sp.dma_start(keep[:, :], dram["chunk_keep"]).then_inc(tables, 16)
            sp.dma_start(one_hot[:, :, :], dram["one_hot"]).then_inc(tables, 16)

        @block.scalar
        def _(act):
            act.activation(k, k, ACT.Sigmoid).then_inc(sigmoids, 1)
            act.activation(q, q, ACT.Silu).then_inc(sigmoids, 1)
            act.wait_ge(gated, 1)
            act.activation(cum[:, :, :], k, ACT.Ln).then_inc(logs, 1)
            act.wait_ge(cum_done, 1)
            act.activation(t.qe[:, :, :], cum[:, :, :], ACT.Exp).then_inc(exps, 1)
            act.activation(t.e_last[:, :, :], steps(cum[:, :, :])[:, :, :, SUB - 1], ACT.Exp).then_inc(exps, 1)
            act.wait_ge(decays, 1)
            act.activation(t.kd[:, :, :], t.kd[:, :, :], ACT.Exp).then_inc(exps, 1)
            for j in range(SUB):
                act.wait_ge(pair_diff, j + 1)
                part = pair[:, j % RING, :, :, 0:SUB - j]
                act.activation(part, part, ACT.Exp).then_inc(pair_exp, 1)

        @block.vector
        def _(dve):
            chain = core.chain(dve, "dve_step")
            dve.wait_ge(sigmoids, 2)
            for h in range(RH):
                last = dve.tensor_scalar(t.fm[:, K + h, :], t.fm[:, K + h, :], t.one_lb[:, h:h + 1], t.lb[:, h:h + 1],
                                         ALU.mult, ALU.add)
                last.then_inc(gated, 1) if h == RH - 1 else chain.link(last)
            dve.wait_ge(logs, 1)
            chain.link(dve.tensor_scalar(k, k, -1.0, 1.0, ALU.mult, ALU.add))
            dve.wait_ge(tables, 32)
            for h in range(RH):
                last = dve.tensor_tensor_scan(cum[:, h, :], keep[:, :], cum[:, h, :], 0.0, ALU.mult, ALU.add)
                last.then_inc(cum_done, 1) if h == RH - 1 else chain.link(last)
            dve.wait_ge(cum_done, 1)
            dve.tensor_tensor(steps(t.kd[:, :, :]), steps(cum[:, :, :])[:, :, :, SUB - 1:SUB].broadcast_to([P, RH, NCH, SUB]),
                              steps(cum[:, :, :]), ALU.subtract).then_inc(decays, 1)
            dve.wait_ge(exps, 3)
            chain.link(dve.tensor_tensor(t.qe[:, :, :], t.qe[:, :, :], q, ALU.mult))
            chain.link(dve.tensor_tensor(t.kd[:, :, :], t.kd[:, :, :], k, ALU.mult))

            def real(ap, a, b):
                return steps(ap)[:, :, 1:NCH, a:b]

            for j in range(SUB):
                n = SUB - j
                part = pair[:, j % RING, :, :, 0:n]
                dve.wait_ge(pair_exp, j + 1)
                chain.link(dve.tensor_tensor(part, part, real(q, j, SUB), ALU.mult))
                dve.tensor_tensor(part, part, real(k, j, j + 1).broadcast_to([P, RH, NCH - 1, n]), ALU.mult)\
                   .then_inc(pair_done, 1)
            dve.wait_ge(pair_used, SUB)
            for h in range(RH):
                dve.tensor_copy(t.within[:, h, :], a_bank[h][:, :]).then_inc(within, 1)

        @block.gpsimd
        def _(pool):
            pool.wait_ge(cum_done, 1)
            for j in range(SUB):
                if j >= RING:
                    pool.wait_ge(pair_used, j - RING + 1)
                n = SUB - j
                pool.tensor_tensor(pair[:, j % RING, :, :, 0:n], steps(cum[:, :, :])[:, :, 1:NCH, j:SUB],
                                   steps(cum[:, :, :])[:, :, 1:NCH, j:j + 1].broadcast_to([P, RH, NCH - 1, n]),
                                   ALU.subtract).then_inc(pair_diff, 1)

        @block.tensor
        def _(pe):
            pe.wait_ge(tables, 32)
            for j in range(SUB):
                n = SUB - j
                pe.wait_ge(pair_done, j + 1)
                for h in range(RH):
                    out = a_bank[h][:, :].rearrange("p (n s) -> p n s", s=SUB)[:, :, j:SUB]
                    last = pe.matmul(out, one_hot[:, j, :], pair[:, j % RING, h, :, 0:n], start=(j == 0), stop=(j == SUB - 1))
                last.then_inc(pair_used, 1)


def gla_scan(core, t, dram):
    nc = core.nc
    W = RH * RK
    VR, STATES = 8, 3
    CT = P // SUB
    with ExitStack() as ctx:
        v_ring = sbuf(nc, ctx, "v_ring", [SUB, VR, W])
        k_ring = sbuf(nc, ctx, "k_ring", [SUB, 2, W])
        rec_t = sbuf(nc, ctx, "rec_t", [P, 2, RH, P])
        state = sbuf(nc, ctx, "state", [P, STATES, RH, RK])
        k_bank = [psum(nc, ctx, f"k_bank{i}", [SUB, W]) for i in range(2)]
        s_bank = [psum(nc, ctx, f"s_bank{i}", [P, W]) for i in range(2)]
        o_bank = [psum(nc, ctx, f"o_bank{i}", [P, RH, SUB]) for i in range(2)]
        back_bank = [psum(nc, ctx, f"back_bank{i}", [P, W]) for i in range(2)]
        v_in = [core.sem(f"v_in{i}") for i in range(VR)]
        k_turned, k_moved, s_summed, s_ready, o_summed, o_moved, turned_back, back_moved = [
            core.sem(f"scan_{n}") for n in ("k_turned", "k_moved", "s_summed", "s_ready", "o_summed", "o_moved",
                                            "turned_back", "back_moved")]
        block = ctx.enter_context(nc.Block())

        @block.sync
        def _(sp):
            for n in range(NCH):
                if n > VR:
                    sp.wait_ge(o_summed, n - VR)
                elif n == VR:
                    sp.wait_ge(s_summed, 1)
                if n == 0:
                    src = t.tm_meta[:, 1, :]
                else:
                    row = (n - 1) * SUB
                    src = t.tm[row % P:row % P + SUB, 1, row // P, :]
                sp.dma_start(v_ring[:, n % VR, :], src).then_inc(v_in[n % VR], 16)

        @block.tensor
        def _(pe):
            def turn_keys(n):
                if n >= 2:
                    pe.wait_ge(k_moved, n - 1)
                for h in range(RH):
                    last = pe.transpose(k_bank[n % 2][:, h * RK:(h + 1) * RK], t.kd[:, h, n * SUB:(n + 1) * SUB], t.ident[:, :])
                last.then_inc(k_turned, 1)

            def state_sums(n):
                pe.wait_ge(v_in[n % VR], 16 * (n // VR + 1))
                pe.wait_ge(k_moved, n + 1)
                if n >= 2:
                    pe.wait_ge(s_ready, n - 1)
                for h in range(RH):
                    w = slice(h * RK, (h + 1) * RK)
                    last = pe.matmul(s_bank[n % 2][:, w], k_ring[:, n % 2, w], v_ring[:, n % VR, w], start=True, stop=True)
                last.then_inc(s_summed, 1)

            def outputs(n):
                if n >= 3:
                    pe.wait_ge(o_moved, n - 2)
                for h in range(RH):
                    out = o_bank[n % 2][:, h, :]
                    pe.matmul(out, v_ring[:, n % VR, h * RK:(h + 1) * RK], t.within[:, h, (n - 1) * SUB:n * SUB],
                              start=True, stop=False)
                    if h == 0:
                        pe.wait_ge(s_ready, n)
                    last = pe.matmul(out, state[:, (n - 1) % STATES, h, :], t.qe[:, h, n * SUB:(n + 1) * SUB],
                                     start=False, stop=True)
                last.then_inc(o_summed, 1)

            def turn_back(tile):
                pe.wait_ge(o_moved, (tile + 1) * CT)
                if tile >= 2:
                    pe.wait_ge(back_moved, tile - 1)
                for h in range(RH):
                    last = pe.transpose(back_bank[tile % 2][:, h * RK:(h + 1) * RK], rec_t[:, tile % 2, h, :], t.ident[:, :])
                last.then_inc(turned_back, 1)

            turn_keys(0)
            turn_keys(1)
            state_sums(0)
            for n in range(1, NCH):
                if n + 1 < NCH:
                    turn_keys(n + 1)
                state_sums(n)
                outputs(n)
                if n > CT and n % CT == 1:
                    turn_back(n // CT - 1)
            turn_back(TT - 1)

        @block.scalar
        def _(act):
            def move_keys(n):
                act.wait_ge(k_turned, n + 1)
                if n >= 2:
                    act.wait_ge(s_summed, n - 1)
                act.activation(k_ring[:, n % 2, :], k_bank[n % 2][:, :], ACT.Copy).then_inc(k_moved, 1)

            def move_back(tile):
                act.wait_ge(turned_back, tile + 1)
                act.activation(t.rec[:, tile, :], back_bank[tile % 2][:, :], ACT.Copy).then_inc(back_moved, 1)

            move_keys(0)
            move_keys(1)
            for n in range(1, NCH):
                if n + 1 < NCH:
                    move_keys(n + 1)
                tile, at = (n - 1) // CT, (n - 1) % CT * SUB
                if tile >= 2:
                    act.wait_ge(turned_back, tile - 1)
                act.wait_ge(o_summed, n)
                act.activation(rec_t[:, tile % 2, :, at:at + SUB], o_bank[n % 2][:, :, :], ACT.Copy).then_inc(o_moved, 1)
                if n > CT and n % CT == 2:
                    move_back(n // CT - 1)
            move_back(TT - 1)

        @block.vector
        def _(dve):
            for n in range(NCH):
                dve.wait_ge(s_summed, n + 1)
                if n == 0:
                    dve.tensor_copy(state[:, 0, :, :].rearrange("p h v -> p (h v)"), s_bank[0][:, :]).then_inc(s_ready, 1)
                    continue
                dve.wait_ge(s_ready, n)
                if n >= STATES:
                    dve.wait_ge(o_summed, n - STATES + 1)
                for h in range(RH):
                    last = dve.scalar_tensor_tensor(state[:, n % STATES, h, :], state[:, (n - 1) % STATES, h, :],
                                                    t.e_last[:, h, n:n + 1], s_bank[n % 2][:, h * RK:(h + 1) * RK],
                                                    ALU.mult, ALU.add)
                last.then_inc(s_ready, 1)


def first_merge(core, t, dram):
    nc = core.nc
    with ExitStack() as ctx:
        w_out = sbuf(nc, ctx, "w_out", [P, 2, KC, BANK])
        feat = sbuf(nc, ctx, "mixed_t", [P, KC, T])
        sq = sbuf(nc, ctx, "head_sq", [P, 2, D])
        ss = sbuf(nc, ctx, "head_ss", [P, TT, KC])
        banks = [psum(nc, ctx, f"merge_bank{i}", [P, BANK]) for i in range(8)]
        w_loaded = [core.sem(f"w_out_in{i}") for i in range(2)]
        squared, ms_ready, rstd_ready, gates, scaled, turned, moved, out_done, out_used, = [
            core.sem(f"merge_{n}") for n in ("squared", "ms", "rstd", "gates", "scaled", "turned", "moved", "out_done", "out_used")]
        sums = core.sem("merge_sums")
        block = ctx.enter_context(nc.Block())

        def half(tile, part):
            return t.mixed[:, tile, :] if part == 0 else t.rec[:, tile, :]

        @block.sync
        def _(sp):
            for c in range(2):
                sp.dma_start(w_out[:, c, :, :], dram["w_out_t"][c]).then_inc(w_loaded[c], 16)

        @block.scalar
        def _(act):
            for tile in range(TT):
                if tile >= 2:
                    act.wait_ge(sums, tile - 1)
                for part in range(2):
                    act.activation(sq[:, tile % 2, part * BANK:(part + 1) * BANK], half(tile, part), ACT.Square)\
                       .then_inc(squared, 1)
            act.activation(t.tm[:, 2, :, :], t.tm[:, 2, :, :], ACT.Silu).then_inc(gates, 1)
            act.wait_ge(ms_ready, 1)
            act.activation(ss[:, :, :], ss[:, :, :], ACT.Sqrt).then_inc(rstd_ready, 1)
            for f in range(KC):
                act.wait_ge(turned, f + 1)
                act.activation(feat[:, f, :], banks[f][:, :], ACT.Copy, scale=t.mixed_scale[:, f:f + 1]).then_inc(moved, 1)

        @block.vector
        def _(dve):
            chain = core.chain(dve, "dve_step")
            for tile in range(TT):
                dve.wait_ge(squared, 2 * tile + 2)
                dve.tensor_reduce(ss[:, tile, :], sq[:, tile % 2, :].rearrange("p (h v) -> p h v", v=P), AX.X, ALU.add)\
                   .then_inc(sums, 1)
            dve.wait_ge(sums, TT)
            chain.link(dve.tensor_scalar(ss[:, :, :], ss[:, :, :], 1.0 / P, EPS, ALU.mult, ALU.add))
            dve.reciprocal(ss[:, :, :], ss[:, :, :]).then_inc(ms_ready, 1)
            dve.wait_ge(rstd_ready, 1)
            dve.wait_ge(gates, 1)
            for tile in range(TT):
                for part in range(2):
                    view = half(tile, part).rearrange("p (h v) -> p h v", v=P)
                    last = dve.tensor_tensor(view, view, ss[:, tile, 4 * part:4 * part + 4].unsqueeze(2)
                                             .broadcast_to([P, 4, P]), ALU.mult)
                    if part == 0:
                        last.then_inc(scaled, 1)
                    else:
                        chain.link(last)
                        dve.tensor_tensor(t.rec[:, tile, :], t.rec[:, tile, :], t.tm[:, 2, tile, :], ALU.mult)\
                           .then_inc(scaled, 1)
            for u in range(2 * TT):
                tile, c = u // 2, u % 2
                dve.wait_ge(out_done, u + 1)
                x = t.x[:, tile, c * BANK:(c + 1) * BANK]
                dve.tensor_tensor(x, x, banks[u][:, :], ALU.add).then_inc(out_used, 1)

        @block.tensor
        def _(pe):
            pe.wait_ge(scaled, 2 * TT)
            for f in range(KC):
                for tile in range(TT):
                    src = half(tile, f // 4)[:, (f % 4) * P:(f % 4 + 1) * P]
                    last = pe.transpose(banks[f][:, tile * P:(tile + 1) * P], src, t.ident[:, :])
                last.then_inc(turned, 1)
            pe.wait_ge(moved, KC)
            for c in range(2):
                pe.wait_ge(w_loaded[c], 16)
            for u in range(2 * TT):
                tile, c = u // 2, u % 2
                for k in range(KC):
                    last = pe.matmul(banks[u][:, :], feat[:, k, tile * P:(tile + 1) * P], w_out[:, c, k, :],
                                     start=(k == 0), stop=(k == KC - 1))
                last.then_inc(out_done, 1)


def norm_rows(core, t, w_dram, src, dst):
    nc = core.nc
    with ExitStack() as ctx:
        w = sbuf(nc, ctx, "rows_w", [P, D])
        sq = sbuf(nc, ctx, "rows_sq", [P, D])
        ss = sbuf(nc, ctx, "rows_ss", [P, TT])
        w_in, squared, ms_ready, rstd_ready, done = [
            Signal(core, f"rows_{n}") for n in ("w_in", "squared", "ms_ready", "rstd_ready", "done")]
        block = ctx.enter_context(nc.Block())

        @block.sync
        def _(sp):
            sp.dma_start(w[:, :], w_dram.broadcast_to([P, D])).then_inc(w_in.handle, 16)

        @block.scalar
        def _(act):
            for tile in range(TT):
                if tile:
                    act.wait_ge(squared.handle, squared.at(tile))
                act.activation(sq[:, :], src[:, tile, :], ACT.Square, accum_out=ss[:, tile:tile + 1])\
                   .then_inc(squared.handle, 1)
            act.wait_ge(ms_ready.handle, ms_ready.at(1))
            act.activation(ss[:, :], ss[:, :], ACT.Sqrt).then_inc(rstd_ready.handle, 1)

        @block.vector
        def _(dve):
            chain = core.chain(dve, "dve_step")
            dve.wait_ge(squared.handle, squared.at(TT))
            chain.link(dve.tensor_scalar(ss[:, :], ss[:, :], 1.0 / D, EPS, ALU.mult, ALU.add))
            dve.reciprocal(ss[:, :], ss[:, :]).then_inc(ms_ready.handle, 1)
            dve.wait_ge(rstd_ready.handle, rstd_ready.at(1))
            dve.wait_ge(w_in.handle, w_in.at(16))
            for tile in range(TT):
                dve.scalar_tensor_tensor(dst[:, tile, :], src[:, tile, :], ss[:, tile:tile + 1], w[:, :],
                                         ALU.mult, ALU.mult).then_inc(done.handle, 1)

        for s, n in ((w_in, 16), (squared, TT), (ms_ready, 1), (rstd_ready, 1), (done, TT)):
            s.used(n)


def peer_load(core, dram, ffn_norm, keys, scores):
    nc = core.nc
    norm_in, pad = core.sem("ffn_norm_in"), core.sem("scores_pad")
    with nc.Block() as block:
        @block.sync
        def _(sp):
            sp.dma_start(ffn_norm[:, :], dram["ffn_norm_cols"]).then_inc(norm_in, 16)
            sp.dma_start(keys[:, :, :], dram["peer_subkeys"]).then_inc(norm_in, 16)
            sp.wait_ge(norm_in, 32)

        @block.vector
        def _(dve):
            dve.memset(scores[:, TT * 2 * PH:, :], 0.0).then_inc(pad, 1)


def peer_queries(core, t, dram, feat, query):
    slabs = [feature_slab(dram["peer_w_query"], b, [(0, T)], b) for b in range(2 * PH)]
    project(core, feat, slabs, [[(query[:, b, :], slice(0, P), slice(0, T))] for b in range(2 * PH)])


def peer_scores(core, t, dram, query, keys, scores):
    nc = core.nc
    QB = 2 * PH
    with ExitStack() as ctx:
        sbank = [psum(nc, ctx, f"sbank{i}", [P, TT, NK]) for i in range(4)]
        s_done, s_moved, s_moved_act = [core.sem(f"peer_{n}") for n in ("s_done", "s_moved", "s_moved_act")]
        block = ctx.enter_context(nc.Block())

        @block.tensor
        def _(pe):
            for b in range(QB):
                if b >= 4:
                    pe.wait_ge(s_moved if b % 2 == 0 else s_moved_act, (b - 4) // 2 + 1)
                for tile in range(TT):
                    last = pe.matmul(sbank[b % 4][:, tile, :], query[:, b, tile * P:(tile + 1) * P], keys[:, b, :],
                                     start=True, stop=True)
                last.then_inc(s_done, 1)

        @block.vector
        def _(dve):
            for b in range(0, QB, 2):
                dve.wait_ge(s_done, b + 1)
                dve.tensor_copy(scores[:, :, b, :], sbank[b % 4][:, :, :]).then_inc(s_moved, 1)

        @block.scalar
        def _(act):
            for b in range(1, QB, 2):
                act.wait_ge(s_done, b + 1)
                act.activation(scores[:, :, b, :], sbank[b % 4][:, :, :], ACT.Copy).then_inc(s_moved_act, 1)


def peer_experts(core, t, dram, hidden, scores):
    nc = core.nc
    RING, PAIRS = 8, PH // 2
    PER = 2 * TOPK
    with ExitStack() as ctx:
        rows = sbuf(nc, ctx, "rows", [P, RING, 2 * D])
        hid = sbuf(nc, ctx, "hid", [P, 3, RING])
        diag = sbuf(nc, ctx, "diag", [P, RING, P])
        zeros = sbuf(nc, ctx, "zeros", [P, BANK])
        step16 = sbuf(nc, ctx, "step16", [P, TOPK])
        s_now = sbuf(nc, ctx, "s_now", [P, 2, NK])
        s_rest = sbuf(nc, ctx, "s_rest", [P, 2, NK])
        top = sbuf(nc, ctx, "top", [P, 2, TOPK])
        top_i = sbuf(nc, ctx, "top_i", [P, 2, TOPK], U32)
        top_f = sbuf(nc, ctx, "top_f", [P, 2, TOPK])
        cand = sbuf(nc, ctx, "cand", [P, TOPK, TOPK])
        cand_rest = sbuf(nc, ctx, "cand_rest", [P, TOPK, TOPK])
        best = sbuf(nc, ctx, "best", [P, TOPK])
        best_i = sbuf(nc, ctx, "best_i", [P, TOPK], U32)
        part_i = sbuf(nc, ctx, "part_i", [P, 2, TOPK], U32)
        part_f = sbuf(nc, ctx, "part_f", [P, 2, TOPK])
        hit = sbuf(nc, ctx, "hit", [P, 2, TOPK, TOPK])
        key = sbuf(nc, ctx, "key", [P, 2, TOPK])
        experts = sbuf(nc, ctx, "experts", [P, 2, TOPK], U32)
        gates = sbuf(nc, ctx, "gates", [P, 2, TOPK])
        soft = sbuf(nc, ctx, "soft", [P, 3, TOPK])
        y = [psum(nc, ctx, f"peer_y{i}", [P, D]) for i in range(2)]
        step_in, ready, go = core.sem("step16_in"), core.sem("zeros_ready"), core.sem("gather_go")
        got = [core.sem(f"rows_in{i}") for i in range(RING)]
        routed, logits, exped, gates_free = [core.sem(f"peer_{n}") for n in ("routed", "logits", "exped", "gates_free")]
        dotted, diag_ready, slot_free, summed, added = [
            core.sem(f"peer_{n}") for n in ("dotted", "diag_ready", "slot_free", "summed", "added")]
        search_go = core.sem("search_go")
        block = ctx.enter_context(nc.Block())

        @block.sync
        def _(sp):
            sp.dma_start(step16[:, :], dram["step16"]).then_inc(step_in, 16)

        @block.gpsimd
        def _(pool):
            for tile in range(TT):
                with pool.Fori(0, PAIRS) as j:
                    for p in range(2):
                        pool.wait_ge(routed, tile * PH + j * 2 + (p + 1))
                        for k in range(TOPK):
                            n = p * TOPK + k
                            pool.wait_ge(slot_free, tile * SLOTS + j * PER + (n + 1))
                            pool.sem_inc(go, 1)
                            pool.indirect_dma_start(rows[:, n % RING, :], None, dram["peer_table"],
                                                    bass.IndirectOffsetOnAxis(ap=experts[:, p, k:k + 1], axis=0))\
                                .then_inc(got[n % RING], 16)

        @block.vector
        def _(dve):
            chain = core.chain(dve, "dve_step")
            dve.memset(zeros[:, :], 0.0).then_inc(ready, 1)
            dve.wait_ge(step_in, 16)
            start = chain.count
            per_route = ROUTE_LINKS

            def route(unit, p):
                link = chain.link
                dve.wait_ge(gates_free, unit + 1)

                def held(instruction):
                    link(instruction)
                    dve.sem_inc(search_go, 1)

                held(dve.tensor_copy(s_now[:, :, :], scores[:, bass.ds(unit * 2, 2), :]))
                for c in range(2):
                    last = dve.max(top[:, c, 0:8], s_now[:, c, :])
                held(last)
                for c in range(2):
                    dve.max_index(top_i[:, c, 0:8], top[:, c, 0:8], s_now[:, c, :])
                    last = dve.match_replace(s_rest[:, c, :], top[:, c, 0:8], s_now[:, c, :], LOWEST)
                held(last)
                for c in range(2):
                    last = dve.max(top[:, c, 8:16], s_rest[:, c, :])
                held(last)
                for c in range(2):
                    last = dve.max_index(top_i[:, c, 8:16], top[:, c, 8:16], s_rest[:, c, :])
                link(last)
                dve.tensor_copy(top_f[:, :, :], top_i[:, :, :])
                held(dve.tensor_tensor(cand[:, :, :], top[:, 0, :].unsqueeze(2).broadcast_to([P, TOPK, TOPK]),
                                       top[:, 1, :].unsqueeze(1).broadcast_to([P, TOPK, TOPK]), ALU.add))
                flat = cand[:, :, :].rearrange("p a b -> p (a b)")
                rest = cand_rest[:, :, :].rearrange("p a b -> p (a b)")
                held(dve.max(best[:, 0:8], flat))
                dve.max_index(best_i[:, 0:8], best[:, 0:8], flat)
                held(dve.match_replace(rest, best[:, 0:8], flat, LOWEST))
                held(dve.max(best[:, 8:16], rest))
                link(dve.max_index(best_i[:, 8:16], best[:, 8:16], rest))
                dve.tensor_scalar(soft[:, 0, :], best[:, :], best[:, 0:1], None, ALU.subtract).then_inc(logits, 1)
                dve.tensor_scalar(part_i[:, 0, :], best_i[:, :], 4, None, ALU.logical_shift_right)
                link(dve.tensor_scalar(part_i[:, 1, :], best_i[:, :], TOPK - 1, None, ALU.bitwise_and))
                link(dve.tensor_copy(part_f[:, :, :], part_i[:, :, :]))
                for c in range(2):
                    last = dve.tensor_tensor(hit[:, c, :, :], part_f[:, c, :].unsqueeze(2).broadcast_to([P, TOPK, TOPK]),
                                             step16[:, :].unsqueeze(1).broadcast_to([P, TOPK, TOPK]), ALU.is_equal)
                link(last)
                for c in range(2):
                    last = dve.tensor_tensor(hit[:, c, :, :], hit[:, c, :, :],
                                             top_f[:, c, :].unsqueeze(1).broadcast_to([P, TOPK, TOPK]), ALU.mult)
                link(last)
                link(dve.tensor_reduce(key[:, :, :], hit[:, :, :, :], AX.X, ALU.add))
                dve.scalar_tensor_tensor(experts[:, p, :], key[:, 0, :], float(NK), key[:, 1, :], ALU.mult, ALU.add)\
                   .then_inc(routed, 1)
                dve.wait_ge(exped, unit + 1)
                link(dve.reduce_sum(soft[:, 2, 0:1], soft[:, 1, :], AX.X))
                link(dve.reciprocal(soft[:, 2, 1:2], soft[:, 2, 0:1]))
                link(dve.tensor_scalar(gates[:, p, :], soft[:, 1, :], soft[:, 2, 1:2], None, ALU.mult))

            def dots(tile, j, p):
                for k in range(TOPK):
                    n = p * TOPK + k
                    b = n % RING
                    dve.wait_ge(got[b], (j * (PER // RING) + (tile * (SLOTS // RING) + n // RING + 1)) * 16)
                    dve.tensor_tensor_reduce(out=rows[:, b, 0:D], in0=rows[:, b, 0:D], in1=hidden[:, tile, :],
                                             scale=1.0, scalar=0.0, op0=ALU.mult, op1=ALU.add,
                                             accum_out=hid[:, 0, b:b + 1]).then_inc(dotted, 1)

            def add_tile(tile):
                dve.wait_ge(summed, tile + 1)
                dve.tensor_tensor(t.x[:, tile, :], t.x[:, tile, :], y[tile % 2][:, :], ALU.add).then_inc(added, 1)

            route(0, 0)
            assert chain.count - start == per_route, (chain.count - start)
            for tile in range(TT):
                with dve.Fori(0, PAIRS) as j:
                    chain.base = j * (2 * per_route)
                    for p in range(2):
                        route(tile * PH + j * 2 + (p + 1), (p + 1) % 2)
                        dots(tile, j, p)
                chain.base = 0
                chain.count += (PAIRS - 1) * 2 * per_route
                if tile >= 1:
                    add_tile(tile - 1)
            add_tile(TT - 1)

        @block.scalar
        def _(act):
            chain = core.chain(act, "act_step")
            act.sem_inc(gates_free, 1)

            def exponentials(unit):
                act.wait_ge(logits, unit + 1)
                act.activation(soft[:, 1, :], soft[:, 0, :], ACT.Exp).then_inc(exped, 1)

            exponentials(0)
            for tile in range(TT):
                with act.Fori(0, PAIRS) as j:
                    chain.base = j * (2 * PER)
                    for p in range(2):
                        act.sem_inc(gates_free, 1)
                        exponentials(tile * PH + j * 2 + (p + 1))
                        for k in range(TOPK):
                            n = p * TOPK + k
                            b = n % RING
                            act.wait_ge(dotted, tile * SLOTS + j * PER + (n + 1))
                            chain.link(act.activation(hid[:, 1, b:b + 1], hid[:, 0, b:b + 1], ACT.Gelu))
                            chain.link(act.activation(hid[:, 2, b:b + 1], hid[:, 1, b:b + 1], ACT.Copy,
                                                      scale=gates[:, p, k:k + 1]))
                            act.activation(diag[:, b, :], t.ident[:, :], ACT.Copy, scale=hid[:, 2, b:b + 1])\
                               .then_inc(diag_ready, 1)
                chain.base = 0
                chain.count += (PAIRS - 1) * 2 * PER

        @block.tensor
        def _(pe):
            pe.sem_inc(slot_free, RING)
            pe.wait_ge(ready, 1)

            def zero(tile, start):
                for c in range(2):
                    last = pe.matmul(y[tile % 2][:, c * BANK:(c + 1) * BANK], t.ident[:, :], zeros[:, :],
                                     start=start, stop=not start)
                return last

            for tile in range(TT):
                if tile >= 2:
                    pe.wait_ge(added, tile - 1)
                zero(tile, True)
                with pe.Fori(0, PAIRS) as j:
                    for n in range(PER):
                        b = n % RING
                        pe.wait_ge(diag_ready, tile * SLOTS + j * PER + (n + 1))
                        for c in range(2):
                            last = pe.matmul(y[tile % 2][:, c * BANK:(c + 1) * BANK], diag[:, b, :],
                                             rows[:, b, D + c * BANK:D + (c + 1) * BANK], start=False, stop=False)
                        last.then_inc(slot_free, 1)
                zero(tile, False).then_inc(summed, 1)


ROUTE_LINKS = 18


def modulation(core, t, dram):
    nc = core.nc
    with ExitStack() as ctx:
        ones = sbuf(nc, ctx, "ones", [P, P])
        norm_w = sbuf(nc, ctx, "norm_w", [P, 3, KC])
        cols = psum(nc, ctx, "mod_cols", [P, 6, KC])
        gate = [psum(nc, ctx, f"mod_gate{i}", [P, D]) for i in range(3)]
        norms_in, ones_ready, cols_done, gates_done = [
            core.sem(f"mod_{n}") for n in ("norms_in", "ones", "cols", "gates")]
        block = ctx.enter_context(nc.Block())

        @block.sync
        def _(sp):
            sp.dma_start(norm_w[:, :, :], dram["norms_2"]).then_inc(norms_in, 16)

        @block.tensor
        def _(pe):
            pe.wait_ge(ones_ready, 1)
            for c, m in enumerate((0, 1, 3, 4, 6, 7)):
                for f in range(KC):
                    col = m * D + f * P
                    last = pe.matmul(cols[:, c, f:f + 1], t.ada_acc[:, col:col + P], ones[:, 0:1], start=True, stop=True)
            last.then_inc(cols_done, 1)
            for g, m in enumerate((2, 5, 8)):
                for half in range(2):
                    col = m * D + half * BANK
                    last = pe.matmul(gate[g][:, half * BANK:(half + 1) * BANK], ones[:, :], t.ada_acc[:, col:col + BANK],
                                     start=True, stop=True)
            last.then_inc(gates_done, 1)

        @block.vector
        def _(dve):
            chain = core.chain(dve, "dve_step")
            dve.memset(ones[:, :], 1.0).then_inc(ones_ready, 1)
            dve.wait_ge(norms_in, 16)
            dve.wait_ge(cols_done, 1)
            both = cols[:, :, :].rearrange("p (m a) f -> p m a f", a=2)
            chain.link(dve.tensor_copy(t.shift[:, :, :], both[:, :, 0, :]))
            chain.link(dve.tensor_scalar(t.scale[:, :, :], both[:, :, 1, :], 1.0, None, ALU.add))
            chain.link(dve.tensor_tensor(t.scale[:, :, :], t.scale[:, :, :], norm_w[:, :, :], ALU.mult))
            dve.wait_ge(gates_done, 1)
            for g, factor in enumerate((0.5, 1.0, 0.5)):
                last = dve.tensor_scalar(t.gate[:, g, :], gate[g][:, :], factor, None, ALU.mult)
            chain.link(last)


def add_product(core, t, act_t, n_blocks, w_rows, gate):
    nc = core.nc
    RAW, RING = 3, 2
    with ExitStack() as ctx:
        w_raw = sbuf(nc, ctx, "down_raw", [P, RAW, D])
        w = Parts(core, ctx, "down_w", [P, RING, D])
        gated = sbuf(nc, ctx, "gated", [P, 2, BANK])
        banks = [psum(nc, ctx, f"down_bank{u}", [P, BANK]) for u in range(2 * TT)]
        w_in = [Signal(core, f"down_in{i}") for i in range(RAW)]
        high, low, used, summed, scaled, added = [
            Signal(core, f"down_{n}") for n in ("high", "low", "used", "summed", "scaled", "added")]
        block = ctx.enter_context(nc.Block())

        @block.sync
        def _(sp):
            for f in range(n_blocks):
                if f >= RAW:
                    sp.wait_ge(low.handle, low.at(f - RAW + 1))
                sp.dma_start(w_raw[:, f % RAW, :], w_rows[f * P:(f + 1) * P, :]).then_inc(w_in[f % RAW].handle, 16)

        @block.scalar
        def _(act):
            for f in range(n_blocks):
                ring = w_in[f % RAW]
                act.wait_ge(ring.handle, ring.at(16 * (f // RAW + 1)))
                if f >= RING:
                    act.wait_ge(used.handle, used.at(f - RING + 1))
                act.activation(w.high[:, f % RING, :], w_raw[:, f % RAW, :], ACT.Copy).then_inc(high.handle, 1)

        @block.tensor
        def _(pe):
            for f in range(n_blocks):
                pe.wait_ge(low.handle, low.at(f + 1))
                for u in range(2 * TT):
                    tile, c = slice((u // 2) * P, (u // 2 + 1) * P), slice((u % 2) * BANK, (u % 2 + 1) * BANK)
                    last = product(pe, banks[u][:, :], (act_t.high[:, f, tile], act_t.low[:, f, tile]),
                                   (w.high[:, f % RING, c], w.low[:, f % RING, c]),
                                   start=(f == 0), stop=(f == n_blocks - 1))
                    if f == n_blocks - 1:
                        last.then_inc(summed.handle, 1)
                if f < n_blocks - 1:
                    last.then_inc(used.handle, 1)

        @block.vector
        def _(dve):
            for f in range(n_blocks):
                dve.wait_ge(high.handle, high.at(f + 1))
                dve.tensor_tensor(w.low[:, f % RING, :], w_raw[:, f % RAW, :], w.high[:, f % RING, :].bitcast(F32),
                                  ALU.subtract).then_inc(low.handle, 1)
            for u in range(2 * TT):
                tile, c = u // 2, u % 2
                cols = slice(c * BANK, (c + 1) * BANK)
                dve.wait_ge(summed.handle, summed.at(u + 1))
                if u >= 2:
                    dve.wait_ge(added.handle, added.at(u - 1))
                dve.tensor_tensor(gated[:, u % 2, :], banks[u][:, :], gate[:, cols], ALU.mult).then_inc(scaled.handle, 1)
                dve.wait_ge(scaled.handle, scaled.at(u + 1))
                dve.tensor_tensor(t.x[:, tile, cols], t.x[:, tile, cols], gated[:, u % 2, :], ALU.add)\
                   .then_inc(added.handle, 1)

        for i, ring in enumerate(w_in):
            ring.used(16 * len(range(i, n_blocks, RAW)))
        for s, n in ((high, n_blocks), (low, n_blocks), (used, n_blocks - 1), (summed, 2 * TT), (scaled, 2 * TT),
                     (added, 2 * TT)):
            s.used(n)


def swiglu(core, t, scale, shift, gate, w_gate, w_up, w_down):
    nc = core.nc
    W = KC * P
    with ExitStack() as outer:
        act_t = Parts(core, outer, "act_t", [P, FB, T])
        with ExitStack() as ctx:
            feat = Parts(core, ctx, "ffn_feat", [P, KC, T])
            norm_to_features(core, t.x, t.ident, feat, scale, bias=shift)
            w_raw = sbuf(nc, ctx, "ffn_raw", [P, 2, 2, W])
            w = Parts(core, ctx, "ffn_w", [P, 2, 2, W])
            silu = sbuf(nc, ctx, "silu", [P, 2, T])
            g_bank = [psum(nc, ctx, f"g_bank{i}", [P, T]) for i in range(2)]
            u_bank = [psum(nc, ctx, f"u_bank{i}", [P, T]) for i in range(2)]
            w_in = [Signal(core, f"ffn_in{i}") for i in range(2)]
            high, low, used, g_done, silu_done, act_full, act_high, act_done = [
                Signal(core, f"ffn_{n}") for n in ("high", "low", "used", "g_done", "silu_done", "act_full", "act_high",
                                                   "act_done")]
            block = ctx.enter_context(nc.Block())

            @block.sync
            def _(sp):
                for f in range(FB):
                    if f >= 2:
                        sp.wait_ge(low.handle, low.at(f - 1))
                    sp.dma_start(w_raw[:, f % 2, 0, :], w_gate[f]).then_inc(w_in[f % 2].handle, 16)
                    sp.dma_start(w_raw[:, f % 2, 1, :], w_up[f]).then_inc(w_in[f % 2].handle, 16)

            @block.tensor
            def _(pe):
                for f in range(FB):
                    b = f % 2
                    pe.wait_ge(low.handle, low.at(f + 1))
                    if f >= 2:
                        pe.wait_ge(act_full.handle, act_full.at(f - 1))
                    for part, bank, done in ((0, g_bank[b], g_done), (1, u_bank[b], used)):
                        for k in range(KC):
                            cols = slice(k * P, (k + 1) * P)
                            last = product(pe, bank[:, :], (w.high[:, b, part, cols], w.low[:, b, part, cols]),
                                           (feat.high[:, k, :], feat.low[:, k, :]), start=(k == 0), stop=(k == KC - 1))
                        last.then_inc(done.handle, 1)

            @block.scalar
            def _(act):
                def weights_high(f):
                    ring = w_in[f % 2]
                    act.wait_ge(ring.handle, ring.at(32 * (f // 2 + 1)))
                    if f >= 2:
                        act.wait_ge(used.handle, used.at(f - 1))
                    act.activation(w.high[:, f % 2, :, :], w_raw[:, f % 2, :, :], ACT.Copy).then_inc(high.handle, 1)

                weights_high(0)
                weights_high(1)
                for f in range(FB):
                    act.wait_ge(g_done.handle, g_done.at(f + 1))
                    if f >= 2:
                        act.wait_ge(act_done.handle, act_done.at(f - 1))
                    act.activation(silu[:, f % 2, :], g_bank[f % 2][:, :], ACT.Silu).then_inc(silu_done.handle, 1)
                    act.wait_ge(act_full.handle, act_full.at(f + 1))
                    act.activation(act_t.high[:, f, :], silu[:, f % 2, :], ACT.Copy).then_inc(act_high.handle, 1)
                    if f + 2 < FB:
                        weights_high(f + 2)

            @block.vector
            def _(dve):
                def weights_low(f):
                    dve.wait_ge(high.handle, high.at(f + 1))
                    dve.tensor_tensor(w.low[:, f % 2, :, :], w_raw[:, f % 2, :, :], w.high[:, f % 2, :, :].bitcast(F32),
                                      ALU.subtract).then_inc(low.handle, 1)

                weights_low(0)
                weights_low(1)
                for f in range(FB):
                    dve.wait_ge(silu_done.handle, silu_done.at(f + 1))
                    dve.wait_ge(used.handle, used.at(f + 1))
                    dve.tensor_tensor(silu[:, f % 2, :], silu[:, f % 2, :], u_bank[f % 2][:, :], ALU.mult)\
                       .then_inc(act_full.handle, 1)
                    if f + 2 < FB:
                        weights_low(f + 2)
                    dve.wait_ge(act_high.handle, act_high.at(f + 1))
                    dve.tensor_tensor(act_t.low[:, f, :], silu[:, f % 2, :], act_t.high[:, f, :].bitcast(F32),
                                      ALU.subtract).then_inc(act_done.handle, 1)

            for ring in w_in:
                ring.used(32 * FB // 2)
            for s in (high, low, used, g_done, silu_done, act_full, act_high, act_done):
                s.used(FB)
        add_product(core, t, act_t, FB, w_down, gate)


def second_projection(core, t, dram, feat, m):
    nc = core.nc
    CB, CR = 12, 4
    slabs, moves = [], []
    rows, cols = slice(0, P), slice(0, BANK)
    tiles = [(tile * P, P) for tile in range(TT)]
    two_pi = 2 * math.pi
    C1 = 6.28125
    C2 = round((two_pi - C1) * 2 ** 21) / 2 ** 21
    C3 = two_pi - C1 - C2
    MAGIC = 1.5 * 2 ** 23
    R = slice(NOPE, QKD)
    SILU, ANGLES, DT, DT_EXP, DT_SUM, DT_LN, SINES, DT_END = CB + 2, CB + 4, CB + 6, CB + 8, CB + 9, CB + 10, CB + 11, CB + 12
    with ExitStack() as ctx:
        conv_in = sbuf(nc, ctx, "conv_in", [P, CR, T + 3])
        conv_w = sbuf(nc, ctx, "conv_w", [P, 4, CB])
        conv_b = sbuf(nc, ctx, "conv_b", [P, CB])
        heads = sbuf(nc, ctx, "heads", [SH, 3])
        keep = sbuf(nc, ctx, "keep2", [SH, T])
        pos_i = sbuf(nc, ctx, "pos_i", [P, T], I32)
        pos = sbuf(nc, ctx, "pos", [P, T])
        turns = sbuf(nc, ctx, "turns", [P, T])
        folded = sbuf(nc, ctx, "folded", [P, T])
        inv = sbuf(nc, ctx, "inv", [P, 1])
        soft = sbuf(nc, ctx, "soft2", [SH, 4, T])
        loads, conv_done, dt_stage, exp_stage, ang_ready = [
            core.sem(f"ssd_{n}") for n in ("loads", "conv", "dt_stage", "exp_stage", "ang_ready")]

        for b in range(CB):
            slabs.append(feature_slab(dram["w_conv"], b, [(0, T)], len(moves)))
            moves.append([(conv_in[:, b % CR, 3:3 + T], rows, cols)])
        slabs.append(feature_slab(dram["w_small"], 0, [(0, T)], len(moves)))
        DT_OUT = len(moves)
        moves.append([(m.dt[:, :], slice(0, SH), cols), (m.k_rope[NOPE:QKD, :], slice(NOPE, QKD), cols)])
        for name, dst, at, width in (("w_z0", m.z, 0, BANK), ("w_z1", m.z, BANK, BANK), ("w_cq", m.latent, 0, QL),
                                     ("w_ckv", m.latent, QL, KVL)):
            slabs += token_slabs(dram[name], tiles, len(moves), width)
            moves += [[(dst[:, tile, at:at + width], rows, slice(0, width))] for tile in range(TT)]

        def beside(block):
            @block.gpsimd
            def _(pool):
                pool.dma_start(conv_w[:, :, :], dram["conv_w_2"]).then_inc(loads, 16)
                pool.dma_start(conv_b[:, :], dram["conv_b_2"]).then_inc(loads, 16)
                pool.dma_start(heads[:, 0:2], dram["ssd_heads"]).then_inc(loads, 16)
                pool.dma_start(keep[:, :], dram["chunk_keep2"]).then_inc(loads, 16)
                pool.dma_start(pos_i[R, :], dram["positions_2"].broadcast_to([ROPE, T])).then_inc(loads, 16)
                pool.dma_start(inv[R, :], dram["rope_inv"]).then_inc(loads, 16)

        def beside_dve(dve, n, moved):
            chain = core.chain(dve, "dve_step")
            link = chain.link
            if n == 0:
                link(dve.memset(conv_in[:, :, 0:3], 0.0))
                dve.wait_ge(loads, 96)
            if 2 <= n < CB + 2:
                b = n - 2
                dve.wait_ge(moved.handle, moved.at(b + 1))
                out = m.conv[:, b, :]
                last = dve.tensor_scalar(out, conv_in[:, b % CR, 0:T], conv_w[:, 0, b:b + 1], conv_b[:, b:b + 1],
                                         ALU.mult, ALU.add)
                for tap in range(1, 4):
                    link(last)
                    last = dve.scalar_tensor_tensor(out, conv_in[:, b % CR, tap:tap + T], conv_w[:, tap, b:b + 1], out,
                                                    ALU.mult, ALU.add)
                last.then_inc(conv_done, 1)
            if n == ANGLES:
                link(dve.tensor_copy(pos[R, :], pos_i[R, :]))
                link(dve.tensor_scalar(pos[R, :], pos[R, :], inv[R, 0:1], None, ALU.mult))
                link(dve.tensor_scalar(turns[R, :], pos[R, :], 1.0 / two_pi, MAGIC, ALU.mult, ALU.add))
                link(dve.tensor_scalar(turns[R, :], turns[R, :], -MAGIC, None, ALU.add))
                for c in (C1, C2, C3):
                    link(dve.scalar_tensor_tensor(pos[R, :], turns[R, :], -c, pos[R, :], ALU.mult, ALU.add))
                link(dve.tensor_scalar(pos[R, :], pos[R, :], -3.1415925, 3.1415925, ALU.max, ALU.min))
                link(dve.tensor_scalar(folded[R, :], pos[R, :], -1.0, None, ALU.mult))
                link(dve.tensor_tensor(folded[R, :], folded[R, :], pos[R, :], ALU.min))
                dve.tensor_scalar(folded[R, :], folded[R, :], math.pi / 2, None, ALU.add).then_inc(ang_ready, 1)
            if n == DT:
                dve.wait_ge(moved.handle, moved.at(DT_OUT + 1))
                link(dve.tensor_scalar(m.dt[:, :], m.dt[:, :], heads[:, 0:1], None, ALU.add))
                link(dve.tensor_scalar(soft[:, 0, :], m.dt[:, :], -1.0, None, ALU.mult))
                dve.tensor_tensor(soft[:, 0, :], soft[:, 0, :], m.dt[:, :], ALU.min).then_inc(dt_stage, 1)
            if n == DT_SUM:
                dve.wait_ge(exp_stage, 2)
                link(dve.tensor_scalar(soft[:, 1, :], soft[:, 0, :], 1.0, None, ALU.add))
                dve.tensor_scalar(soft[:, 2, :], soft[:, 1, :], -1.0, None, ALU.add).then_inc(dt_stage, 1)
            if n == DT_END:
                dve.wait_ge(dt_stage, 2)
                link(dve.tensor_tensor(soft[:, 2, :], soft[:, 0, :], soft[:, 2, :], ALU.subtract))
                dve.wait_ge(exp_stage, 3)
                link(dve.reciprocal(soft[:, 1, :], soft[:, 1, :]))
                link(dve.tensor_tensor(soft[:, 2, :], soft[:, 2, :], soft[:, 1, :], ALU.mult))
                link(dve.tensor_tensor(soft[:, 2, :], soft[:, 2, :], soft[:, 3, :], ALU.add))
                link(dve.scalar_tensor_tensor(m.dt[:, :], m.dt[:, :], 0.0, soft[:, 2, :], ALU.max, ALU.add))
                link(dve.tensor_scalar(soft[:, 0, :], m.dt[:, :], heads[:, 2:3], -1.0, ALU.mult, ALU.mult))
                link(dve.tensor_tensor_scan(m.a_cum[:, :], keep[:, :], soft[:, 0, :], 0.0, ALU.mult, ALU.add))

        def before_moves(act, n):
            if CR <= n < CB:
                act.wait_ge(conv_done, n - CR + 1)

        def beside_act(act, n):
            if SILU <= n < SILU + CB // 2:
                for b in (2 * (n - SILU), 2 * (n - SILU) + 1):
                    act.wait_ge(conv_done, b + 1)
                    act.activation(m.conv[:, b, :], m.conv[:, b, :], ACT.Silu)
            if n == DT_EXP:
                act.wait_ge(dt_stage, 1)
                act.activation(soft[:, 0, :], soft[:, 0, :], ACT.Exp).then_inc(exp_stage, 1)
                act.activation(heads[:, 2:3], heads[:, 1:2], ACT.Exp).then_inc(exp_stage, 1)
            if n == DT_LN:
                act.wait_ge(dt_stage, 2)
                act.activation(soft[:, 3, :], soft[:, 1, :], ACT.Ln).then_inc(exp_stage, 1)
            if n == SINES:
                act.wait_ge(ang_ready, 1)
                act.activation(m.sin[R, :], pos[R, :], ACT.Sin)
                act.activation(m.cos[R, :], folded[R, :], ACT.Sin)

        project(core, feat, slabs, moves, beside, beside_dve, before_moves, beside_act)


def ssd_prepare(core, t, dram, m):
    nc = core.nc
    XB = 8
    with ExitStack() as ctx:
        pick = sbuf(nc, ctx, "pick", [SH, SH, P])
        mask = sbuf(nc, ctx, "mask_t", [P, P])
        a_last = sbuf(nc, ctx, "a_last", [P, TT, SH])
        a_tok = sbuf(nc, ctx, "a_tok", [P, TT, 2, SH])
        to_end = sbuf(nc, ctx, "to_end", [P, TT, SH])
        bank = [psum(nc, ctx, f"prep_bank{i}", [P, BANK]) for i in range(4)]
        row_bank = [psum(nc, ctx, f"row_bank{i}", [P, TT, P]) for i in range(2)]
        small = psum(nc, ctx, "prep_small", [P, TT, 2, SH])
        consts, turned, moved, moved_act, small_done, cb_done, cb_moved, rows_done, rows_used = [
            core.sem(f"prep_{n}") for n in ("consts", "turned", "moved", "moved_act", "small", "cb", "cb_moved", "rows",
                                            "rows_used")]
        diffs, exps, small_moved, ends, ends_exp, small_exp = [
            core.sem(f"prep_{n}") for n in ("diffs", "exps", "small_moved", "ends", "ends_exp", "small_exp")]
        block = ctx.enter_context(nc.Block())

        @block.sync
        def _(sp):
            sp.dma_start(pick[:, :, :], dram["pick"]).then_inc(consts, 16)
            sp.dma_start(mask[:, :], dram["causal_t"]).then_inc(consts, 16)
            sp.dma_start(m.d_skip[:, :], dram["d_skip_2"].broadcast_to([P, SH])).then_inc(consts, 16)

        def turn(pe, b):
            if b < 2:
                pe.wait_ge(cb_moved, SG)
            if b >= 2:
                pe.wait_ge(moved_act, b - 1)
            for tile in range(TT):
                last = pe.transpose(bank[b % 2][:, tile * P:(tile + 1) * P], m.conv[:, b, tile * P:(tile + 1) * P],
                                    t.ident[:, :])
            last.then_inc(turned, 1)

        @block.tensor
        def _(pe):
            for tile in range(TT):
                cols = slice(tile * P, (tile + 1) * P)
                pe.transpose(small[:, tile, 0, :], m.dt[:, cols], t.ident[0:SH, 0:SH])
                last = pe.transpose(small[:, tile, 1, :], m.a_cum[:, cols], t.ident[0:SH, 0:SH])
            last.then_inc(small_done, 1)
            for g in range(SG):
                for c in range(TT):
                    cols = slice(c * P, (c + 1) * P)
                    last = pe.matmul(bank[g][:, cols], m.conv[:, XB + g, cols], m.conv[:, XB + SG + g, cols],
                                     start=True, stop=True)
                last.then_inc(cb_done, 1)
            pe.wait_ge(consts, 48)
            for r in range(SH):
                if r >= 2:
                    pe.wait_ge(rows_used, r - 1)
                pe.matmul(row_bank[r % 2][:, :, :].rearrange("p c s -> p (c s)"), pick[:, r, :], m.a_cum[:, :],
                          start=True, stop=True).then_inc(rows_done, 1)
                if r >= 6:
                    turn(pe, r - 6)

        def masked(dve, r):
            dve.wait_ge(exps, r + 1)
            dve.tensor_tensor(m.between[:, r, :, :], m.between[:, r, :, :], m.cb[:, r // HPG, :, :], ALU.mult)\
               .then_inc(diffs, 1)

        @block.vector
        def _(dve):
            chain = core.chain(dve, "dve_step")
            link = chain.link
            dve.wait_ge(small_done, 1)
            dve.tensor_copy(a_tok[:, :, :, :], small[:, :, :, :]).then_inc(small_moved, 1)
            dve.wait_ge(small_moved, 1)
            dve.wait_ge(consts, 48)
            for g in range(SG):
                dve.wait_ge(cb_done, g + 1)
                dve.tensor_tensor(m.cb[:, g, :, :], bank[g][:, :].rearrange("p (c s) -> p c s", c=TT),
                                  mask[:, :].unsqueeze(1).broadcast_to([P, TT, P]), ALU.mult).then_inc(cb_moved, 1)
            for r in range(SH):
                dve.wait_ge(rows_done, r + 1)
                dve.tensor_copy(a_last[:, :, r], row_bank[r % 2][:, :, P - 1])
                for c in range(TT):
                    last = dve.tensor_scalar(m.between[:, r, c, :], row_bank[r % 2][:, c, :], a_tok[:, c, 1, r:r + 1],
                                             0.0, ALU.subtract, ALU.min)
                last.then_inc(rows_used, 1)
                if r >= 1:
                    masked(dve, r - 1)
            masked(dve, SH - 1)
            dve.wait_ge(rows_used, SH)
            dve.tensor_tensor(to_end[:, :, :], a_last[:, :, :], a_tok[:, :, 1, :], ALU.subtract).then_inc(ends, 1)
            dve.wait_ge(ends_exp, 1)
            dve.wait_ge(moved_act, XB + SG)
            def by_head(ap):
                return ap.rearrange("p (r d) -> p r d", d=SHD)
            for c in range(TT):
                link(dve.tensor_tensor(by_head(m.x_dt[:, c, :]), by_head(m.x_tok[:, c, :]),
                                       a_tok[:, c, 0, :].unsqueeze(2).broadcast_to([P, SH, SHD]), ALU.mult))
                link(dve.tensor_tensor(by_head(m.x_end[:, c, :]), by_head(m.x_dt[:, c, :]),
                                       to_end[:, c, :].unsqueeze(2).broadcast_to([P, SH, SHD]), ALU.mult))

        def move(act, b):
            act.wait_ge(turned, b + 1)
            src = bank[b % 2][:, :].rearrange("p (c s) -> p c s", c=TT)
            dst = m.x_tok[:, :, b * P:(b + 1) * P] if b < XB else m.b_tok[:, :, b - XB, :]
            act.activation(dst, src, ACT.Copy).then_inc(moved_act, 1)

        @block.scalar
        def _(act):
            act.wait_ge(small_moved, 1)
            act.activation(m.e_cum[:, :, :], a_tok[:, :, 1, :], ACT.Exp)
            for r in range(SH):
                act.wait_ge(rows_used, r + 1)
                act.activation(m.between[:, r, :, :], m.between[:, r, :, :], ACT.Exp).then_inc(exps, 1)
                if r >= 6:
                    move(act, r - 6)
            act.wait_ge(ends, 1)
            act.activation(m.e_last[:, :, :], a_last[:, :, :], ACT.Exp)
            act.activation(to_end[:, :, :], to_end[:, :, :], ACT.Exp).then_inc(ends_exp, 1)


def ssd_chunks(core, t, dram, m):
    nc = core.nc
    G = HPG * SHD
    with ExitStack() as ctx:
        state = sbuf(nc, ctx, "ssd_state", [P, 2, SG, G])
        carried = sbuf(nc, ctx, "carried", [P, D])
        y_bank = [psum(nc, ctx, f"y_bank{i}", [P, D]) for i in range(2)]
        c_bank = psum(nc, ctx, "carry_bank", [P, D])
        s_bank = psum(nc, ctx, "state_bank", [P, D])
        diag_done, carry_done, state_done, state_ready, y_used, carry_used = [
            core.sem(f"chunk_{n}") for n in ("diag", "carry", "state", "state_ready", "y_used", "carry_used")]
        block = ctx.enter_context(nc.Block())

        @block.tensor
        def _(pe):
            for c in range(TT):
                if c >= 2:
                    pe.wait_ge(y_used, c - 1)
                for r in range(SH):
                    w = slice(r * SHD, (r + 1) * SHD)
                    last = pe.matmul(y_bank[c % 2][:, w], m.between[:, r, c, :], m.x_dt[:, c, w], start=True, stop=True)
                last.then_inc(diag_done, 1)
                if c < TT - 1:
                    if c >= 1:
                        pe.wait_ge(state_ready, c)
                    for g in range(SG):
                        last = pe.matmul(s_bank[:, g * G:(g + 1) * G], m.b_tok[:, c, g, :], m.x_end[:, c, g * G:(g + 1) * G],
                                         start=True, stop=True)
                    last.then_inc(state_done, 1)
                if c >= 1:
                    pe.wait_ge(state_ready, c)
                    if c >= 2:
                        pe.wait_ge(carry_used, c - 1)
                    for g in range(SG):
                        last = pe.matmul(c_bank[:, g * G:(g + 1) * G], m.conv[:, 10 + g, c * P:(c + 1) * P],
                                         state[:, c % 2, g, :], start=True, stop=True)
                    last.then_inc(carry_done, 1)

        @block.vector
        def _(dve):
            chain = core.chain(dve, "dve_step")
            link = chain.link

            def by_head(ap):
                return ap.rearrange("p (r d) -> p r d", d=SHD)

            for c in range(TT):
                if c < TT - 1:
                    dve.wait_ge(state_done, c + 1)
                    new = state[:, (c + 1) % 2, :, :].rearrange("p g w -> p (g w)")
                    if c == 0:
                        dve.tensor_copy(new, s_bank[:, :]).then_inc(state_ready, 1)
                    else:
                        old = state[:, c % 2, :, :].rearrange("p g w -> p (g w)")
                        dve.wait_ge(carry_done, c - 1) if c >= 2 else None
                        link(dve.tensor_tensor(by_head(new), by_head(old),
                                               m.e_last[:, c, :].unsqueeze(2).broadcast_to([P, SH, SHD]), ALU.mult))
                        dve.tensor_tensor(new, new, s_bank[:, :], ALU.add).then_inc(state_ready, 1)
                dve.wait_ge(diag_done, c + 1)
                y = m.y[:, c, :]
                link(dve.tensor_tensor(by_head(y), by_head(m.x_tok[:, c, :]),
                                       m.d_skip[:, :].unsqueeze(2).broadcast_to([P, SH, SHD]), ALU.mult))
                last = dve.tensor_tensor(y, y, y_bank[c % 2][:, :], ALU.add)
                last.then_inc(y_used, 1)
                dve.wait_ge(y_used, c + 1)
                if c >= 1:
                    dve.wait_ge(carry_done, c)
                    dve.tensor_tensor(by_head(carried[:, :]), by_head(c_bank[:, :]),
                                      m.e_cum[:, c, :].unsqueeze(2).broadcast_to([P, SH, SHD]), ALU.mult)\
                       .then_inc(carry_used, 1)
                    dve.wait_ge(carry_used, c)
                    link(dve.tensor_tensor(y, y, carried[:, :], ALU.add))


def mla_projection(core, t, dram, m, a):
    nc = core.nc
    QK3, KV2 = QL // P, KVL // P
    R = slice(NOPE, QKD)
    with ExitStack() as ctx:
        w_q = sbuf(nc, ctx, "w_q", [P, MH, QK3 * QKD])
        w_k = sbuf(nc, ctx, "w_k", [P, MH, KV2 * NOPE])
        w_v = sbuf(nc, ctx, "w_v", [P, 2, KV2, BANK])
        lat_norm = sbuf(nc, ctx, "lat_norm", [P, QK3 + KV2])
        turn = sbuf(nc, ctx, "turn2", [P, ROPE])
        sq = sbuf(nc, ctx, "lat_sq", [P, QL])
        ss = sbuf(nc, ctx, "lat_ss", [P, 2, TT])
        lat_t = sbuf(nc, ctx, "lat_t", [P, QK3 + KV2, T])
        swung = sbuf(nc, ctx, "swung2", [P, 2, T])
        bank = [psum(nc, ctx, f"mla_bank{i}", [P, BANK]) for i in range(8)]
        loads, squared, ms_ready, rstd, scaled, turned, moved, projected, proj_moved = [
            core.sem(f"mla_{n}") for n in ("loads", "squared", "ms", "rstd", "scaled", "turned", "moved", "projected",
                                           "proj_moved")]
        rot_done, swung_done, rotated, = [core.sem(f"mla_{n}") for n in ("rot_done", "swung", "rotated")]
        block = ctx.enter_context(nc.Block())
        NB = QK3 + KV2
        units = [("q", h, 0) for h in range(MH)] + [("k", h, 0) for h in range(MH)] + \
                [("v", tile, c) for tile in range(TT) for c in range(2)]

        @block.sync
        def _(sp):
            sp.dma_start(w_q[:, :, :], dram["w_uq_2"]).then_inc(loads, 16)
            sp.dma_start(w_k[:, :, :], dram["w_uk"]).then_inc(loads, 16)
            sp.dma_start(w_v[:, :, :, :], dram["w_uv"]).then_inc(loads, 16)
            sp.dma_start(lat_norm[:, :], dram["latent_norm"]).then_inc(loads, 16)
            sp.dma_start(turn[R, :], dram["rope_turn2"]).then_inc(loads, 16)

        @block.scalar
        def _(act):
            n = 0
            for part, (lo, hi) in enumerate(((0, QL), (QL, QL + KVL))):
                for tile in range(TT):
                    if n:
                        act.wait_ge(squared, n)
                    n += 1
                    act.activation(sq[:, 0:hi - lo], m.latent[:, tile, lo:hi], ACT.Square,
                                   accum_out=ss[:, part, tile:tile + 1]).then_inc(squared, 1)
            act.wait_ge(ms_ready, 1)
            act.activation(ss[:, :, :], ss[:, :, :], ACT.Sqrt).then_inc(rstd, 1)
            act.wait_ge(loads, 80)
            for f in range(NB):
                act.wait_ge(turned, f + 1)
                act.activation(lat_t[:, f, :], bank[f][:, :], ACT.Copy, scale=lat_norm[:, f:f + 1]).then_inc(moved, 1)
            for u, (kind, i, c) in enumerate(units):
                act.wait_ge(projected, u + 1)
                if kind == "q":
                    act.activation(a.q[:, i, :], bank[u % 5][0:QKD, :], ACT.Copy).then_inc(proj_moved, 1)
                elif kind == "k":
                    act.activation(a.k[0:NOPE, i, :], bank[u % 5][0:NOPE, :], ACT.Copy).then_inc(proj_moved, 1)
                else:
                    act.activation(a.v[:, i, c * BANK:(c + 1) * BANK], bank[u % 5][:, :], ACT.Copy).then_inc(proj_moved, 1)

        @block.vector
        def _(dve):
            chain = core.chain(dve, "dve_step")
            link = chain.link
            dve.wait_ge(squared, 2 * TT)
            link(dve.tensor_scalar(ss[:, 0, :], ss[:, 0, :], 1.0 / QL, EPS, ALU.mult, ALU.add))
            link(dve.tensor_scalar(ss[:, 1, :], ss[:, 1, :], 1.0 / KVL, EPS, ALU.mult, ALU.add))
            dve.reciprocal(ss[:, :, :], ss[:, :, :]).then_inc(ms_ready, 1)
            dve.wait_ge(rstd, 1)
            for tile in range(TT):
                for part, (lo, hi) in enumerate(((0, QL), (QL, QL + KVL))):
                    dve.tensor_scalar(m.latent[:, tile, lo:hi], m.latent[:, tile, lo:hi], ss[:, part, tile:tile + 1],
                                      None, ALU.mult).then_inc(scaled, 1)
            for n in range(MH + 1):
                ap = m.k_rope[R, :] if n == 0 else a.q[R, n - 1, :]
                dve.wait_ge(rot_done, n + 1)
                dve.tensor_tensor(swung[R, n % 2, :], bank[5 + n % 2][R, :], m.sin[R, :], ALU.mult).then_inc(swung_done, 1)
                link(dve.tensor_tensor(ap, ap, m.cos[R, :], ALU.mult))
                dve.wait_ge(swung_done, n + 1)
                dve.tensor_tensor(ap, ap, swung[R, n % 2, :], ALU.add).then_inc(rotated, 1)

        @block.gpsimd
        def _(pool):
            pool.wait_ge(rotated, 1)
            for h in range(MH):
                pool.tensor_copy(a.k[R, h, :], m.k_rope[R, :])

        @block.tensor
        def _(pe):
            pe.wait_ge(scaled, 2 * TT)
            for f in range(NB):
                for tile in range(TT):
                    last = pe.transpose(bank[f][:, tile * P:(tile + 1) * P], m.latent[:, tile, f * P:(f + 1) * P],
                                        t.ident[:, :])
                last.then_inc(turned, 1)
            pe.wait_ge(loads, 80)

            def rotate(n):
                if n >= 1:
                    pe.wait_ge(proj_moved, n)
                if n >= 2:
                    pe.wait_ge(swung_done, n - 1)
                ap = m.k_rope[R, :] if n == 0 else a.q[R, n - 1, :]
                pe.matmul(bank[5 + n % 2][R, :], turn[R, :], ap, start=True, stop=True).then_inc(rot_done, 1)

            pe.wait_ge(moved, NB)
            rotate(0)
            for u, (kind, i, c) in enumerate(units):
                if u >= 5:
                    pe.wait_ge(proj_moved, u - 4)
                b = bank[u % 5]
                if kind == "q":
                    for k in range(QK3):
                        last = pe.matmul(b[0:QKD, :], w_q[:, i, k * QKD:(k + 1) * QKD], lat_t[:, k, :],
                                         start=(k == 0), stop=(k == QK3 - 1))
                elif kind == "k":
                    for k in range(KV2):
                        last = pe.matmul(b[0:NOPE, :], w_k[:, i, k * NOPE:(k + 1) * NOPE], lat_t[:, QK3 + k, :],
                                         start=(k == 0), stop=(k == KV2 - 1))
                else:
                    for k in range(KV2):
                        last = pe.matmul(b[:, :], lat_t[:, QK3 + k, i * P:(i + 1) * P], w_v[:, c, k, :],
                                         start=(k == 0), stop=(k == KV2 - 1))
                last.then_inc(projected, 1)
                if 2 <= u < MH + 2:
                    rotate(u - 1)


def mla_attention(core, t, dram, m, a):
    nc = core.nc
    scale = 1.0 / math.sqrt(QKD)
    units = [(h, i) for h in range(MH) for i in range(TT)]
    N = len(units)
    with ExitStack() as ctx:
        mask = sbuf(nc, ctx, "mask2", [P, P])
        prob = sbuf(nc, ctx, "prob2", [P, 2, T])
        p_turned = sbuf(nc, ctx, "p_turned", [P, 2, TT, P])
        stat = sbuf(nc, ctx, "stat2", [P, 2, 4])
        score = [psum(nc, ctx, f"score2_{i}", [P, T]) for i in range(2)]
        turn_bank = [psum(nc, ctx, f"turn2_bank{i}", [P, TT, P]) for i in range(2)]
        out_bank = [psum(nc, ctx, f"out2_bank{i}", [P, MV]) for i in range(2)]
        mask_in, scored, max_ready, exp_done, turned, turned_moved, summed, out_moved = [
            core.sem(f"mat_{n}") for n in ("mask_in", "scored", "max", "exp", "turned", "turned_moved", "summed", "out_moved")]
        block = ctx.enter_context(nc.Block())

        @block.sync
        def _(sp):
            sp.dma_start(mask[:, :], dram["causal"]).then_inc(mask_in, 16)

        @block.tensor
        def _(pe):
            def scores(u):
                h, i = units[u]
                if u >= 2:
                    pe.wait_ge(exp_done, u - 1)
                pe.matmul(score[u % 2][:, 0:(i + 1) * P], a.q[:, h, i * P:(i + 1) * P], a.k[:, h, 0:(i + 1) * P],
                          start=True, stop=True).then_inc(scored, 1)

            def turn(u):
                i = units[u][1]
                pe.wait_ge(exp_done, u + 1)
                if u >= 2:
                    pe.wait_ge(turned_moved, u - 1)
                for j in range(i + 1):
                    last = pe.transpose(turn_bank[u % 2][:, j, :], prob[:, u % 2, j * P:(j + 1) * P], t.ident[:, :])
                last.then_inc(turned, 1)

            def values(u):
                h, i = units[u]
                pe.wait_ge(turned_moved, u + 1)
                if u >= 2:
                    pe.wait_ge(out_moved, u - 1)
                for j in range(i + 1):
                    last = pe.matmul(out_bank[u % 2][:, :], p_turned[:, u % 2, j, :], a.v[:, j, h * MV:(h + 1) * MV],
                                     start=(j == 0), stop=(j == i))
                last.then_inc(summed, 1)

            scores(0)
            for u in range(N):
                if u + 1 < N:
                    scores(u + 1)
                if u >= 1:
                    values(u - 1)
                turn(u)
            values(N - 1)

        def out(act, u):
            i = units[u][1]
            act.wait_ge(turned, u + 1)
            if u >= 2:
                act.wait_ge(summed, u - 1)
            act.activation(p_turned[:, u % 2, 0:i + 1, :], turn_bank[u % 2][:, 0:i + 1, :], ACT.Copy)\
               .then_inc(turned_moved, 1)

        @block.scalar
        def _(act):
            for u, (h, i) in enumerate(units):
                n = (i + 1) * P
                act.wait_ge(max_ready, u + 1)
                if u >= 2:
                    act.wait_ge(turned, u - 1)
                act.activation(prob[:, u % 2, 0:n], score[u % 2][:, 0:n], ACT.Exp, bias=stat[:, u % 2, 1:2], scale=scale,
                               accum_out=stat[:, u % 2, 2:3]).then_inc(exp_done, 1)
                if u >= 1:
                    out(act, u - 1)
            out(act, N - 1)

        @block.vector
        def _(dve):
            chain = core.chain(dve, "dve_step")
            link = chain.link
            dve.wait_ge(mask_in, 16)

            def finish(u):
                h, i = units[u]
                dve.wait_ge(exp_done, u + 1)
                link(dve.reciprocal(stat[:, u % 2, 3:4], stat[:, u % 2, 2:3]))
                dve.wait_ge(summed, u + 1)
                dve.tensor_scalar(a.out[:, i, h * MV:(h + 1) * MV], out_bank[u % 2][:, :], stat[:, u % 2, 3:4], None,
                                  ALU.mult).then_inc(out_moved, 1)

            for u, (h, i) in enumerate(units):
                n = (i + 1) * P
                dve.wait_ge(scored, u + 1)
                if u >= 2:
                    finish(u - 2)
                diag = score[u % 2][:, i * P:(i + 1) * P]
                link(dve.tensor_tensor(diag, diag, mask[:, :], ALU.add))
                link(dve.reduce_max(stat[:, u % 2, 0:1], score[u % 2][:, 0:n], AX.X))
                dve.tensor_scalar(stat[:, u % 2, 1:2], stat[:, u % 2, 0:1], -scale, None, ALU.mult).then_inc(max_ready, 1)
            finish(N - 2)
            finish(N - 1)


def mix_features(core, t, dram, m, a, feat):
    nc = core.nc
    with ExitStack() as ctx:
        norm = sbuf(nc, ctx, "mix_w", [P, 2 * KC])
        sq = sbuf(nc, ctx, "mix_sq", [P, D])
        full = sbuf(nc, ctx, "mix_full", [P, 4, T])
        ss = sbuf(nc, ctx, "mix_ss", [P, TT, 3])
        banks = [psum(nc, ctx, f"mix_bank{i}", [P, BANK]) for i in range(8)]
        norm_in, silus, gated, squared, ms_ready, rstd, scaled, turned, whole, high, low = [
            core.sem(f"mix_{n}") for n in ("norm_in", "silus", "gated", "squared", "ms", "rstd", "scaled", "turned",
                                           "whole", "high", "low")]
        block = ctx.enter_context(nc.Block())
        H = D // 2

        @block.sync
        def _(sp):
            sp.dma_start(norm[:, :], dram["mix_norm_2"]).then_inc(norm_in, 16)

        @block.scalar
        def _(act):
            for tile in range(TT):
                act.activation(m.z[:, tile, :], m.z[:, tile, :], ACT.Silu).then_inc(silus, 1)
            n = 0
            for tile in range(TT):
                for part, src in enumerate((m.y[:, tile, 0:H], m.y[:, tile, H:D], a.out[:, tile, :])):
                    if part < 2:
                        act.wait_ge(gated, tile + 1)
                    if n:
                        act.wait_ge(squared, n)
                    n += 1
                    act.activation(sq[:, 0:D if part == 2 else H], src, ACT.Square,
                                   accum_out=ss[:, tile, part:part + 1]).then_inc(squared, 1)
            act.wait_ge(ms_ready, 1)
            act.activation(ss[:, :, :], ss[:, :, :], ACT.Sqrt).then_inc(rstd, 1)
            for f in range(2 * KC):
                act.wait_ge(whole, f + 1)
                act.activation(feat.high[:, f, :], full[:, f % 4, :], ACT.Copy).then_inc(high, 1)

        @block.vector
        def _(dve):
            chain = core.chain(dve, "dve_step")
            link = chain.link
            for tile in range(TT):
                dve.wait_ge(silus, tile + 1)
                dve.tensor_tensor(m.y[:, tile, :], m.y[:, tile, :], m.z[:, tile, :], ALU.mult).then_inc(gated, 1)
            dve.wait_ge(squared, 3 * TT)
            link(dve.tensor_scalar(ss[:, :, 0:2], ss[:, :, 0:2], 1.0 / H, EPS, ALU.mult, ALU.add))
            link(dve.tensor_scalar(ss[:, :, 2:3], ss[:, :, 2:3], 1.0 / D, EPS, ALU.mult, ALU.add))
            dve.reciprocal(ss[:, :, :], ss[:, :, :]).then_inc(ms_ready, 1)
            dve.wait_ge(rstd, 1)
            for tile in range(TT):
                for part, ap in enumerate((m.y[:, tile, 0:H], m.y[:, tile, H:D], a.out[:, tile, :])):
                    dve.tensor_scalar(ap, ap, ss[:, tile, part:part + 1], None, ALU.mult).then_inc(scaled, 1)
            dve.wait_ge(norm_in, 16)
            for f in range(2 * KC + 1):
                if f < 2 * KC:
                    dve.wait_ge(turned, f + 1)
                    if f >= 4:
                        dve.wait_ge(low, f - 3)
                    dve.tensor_scalar(full[:, f % 4, :], banks[f % 8][:, :], norm[:, f:f + 1], None, ALU.mult)\
                       .then_inc(whole, 1)
                if f >= 1:
                    dve.wait_ge(high, f)
                    dve.tensor_tensor(feat.low[:, f - 1, :], full[:, (f - 1) % 4, :], feat.high[:, f - 1, :].bitcast(F32),
                                      ALU.subtract).then_inc(low, 1)

        @block.tensor
        def _(pe):
            pe.wait_ge(scaled, 3 * TT)
            for f in range(2 * KC):
                if f >= 8:
                    pe.wait_ge(whole, f - 7)
                src = m.y if f < KC else a.out
                for tile in range(TT):
                    last = pe.transpose(banks[f % 8][:, tile * P:(tile + 1) * P], src[:, tile, (f % KC) * P:(f % KC + 1) * P],
                                        t.ident[:, :])
                last.then_inc(turned, 1)


def second_mixer(core, t, dram):
    nc = core.nc
    m, a = Tensors(), Tensors()
    with ExitStack() as outer:
        m.z = sbuf(nc, outer, "z", [P, TT, D])
        m.latent = sbuf(nc, outer, "latent", [P, TT, QL + KVL])
        m.k_rope = sbuf(nc, outer, "k_rope", [P, T])
        m.sin = sbuf(nc, outer, "sin2", [P, T])
        m.cos = sbuf(nc, outer, "cos2", [P, T])
        m.y = sbuf(nc, outer, "y_ssd", [P, TT, D])
        with ExitStack() as ssd:
            m.dt = sbuf(nc, ssd, "dt", [SH, T])
            m.a_cum = sbuf(nc, ssd, "a_cum", [SH, T])
            m.conv = sbuf(nc, ssd, "conv", [P, 12, T])
            with ExitStack() as ctx:
                feat = Parts(core, ctx, "mix_feat", [P, KC, T])
                norm_to_features(core, t.x, t.ident, feat, t.scale[:, 1, :], bias=t.shift[:, 1, :])
                second_projection(core, t, dram, feat, m)
            m.d_skip = sbuf(nc, ssd, "d_skip", [P, SH])
            m.between = sbuf(nc, ssd, "between", [P, SH, TT, P])
            m.cb = sbuf(nc, ssd, "cb", [P, SG, TT, P])
            m.x_tok = sbuf(nc, ssd, "x_tok", [P, TT, D])
            m.x_dt = sbuf(nc, ssd, "x_dt", [P, TT, D])
            m.x_end = sbuf(nc, ssd, "x_end", [P, TT, D])
            m.b_tok = sbuf(nc, ssd, "b_tok", [P, TT, SG, SN])
            m.e_cum = sbuf(nc, ssd, "e_cum", [P, TT, SH])
            m.e_last = sbuf(nc, ssd, "e_last2", [P, TT, SH])
            ssd_prepare(core, t, dram, m)
            ssd_chunks(core, t, dram, m)
        a.out = sbuf(nc, outer, "mla_out", [P, TT, D])
        with ExitStack() as mla:
            a.q = sbuf(nc, mla, "mla_q", [QKD, MH, T])
            a.k = sbuf(nc, mla, "mla_k", [QKD, MH, T])
            a.v = sbuf(nc, mla, "mla_v", [P, TT, D])
            mla_projection(core, t, dram, m, a)
            mla_attention(core, t, dram, m, a)
        feat = Parts(core, outer, "mixed_feat", [P, 2 * KC, T])
        mix_features(core, t, dram, m, a, feat)
        add_product(core, t, feat, 2 * KC, dram["w_out_2"][0], t.gate[:, 1, :])


class Tensors:
    pass


def store(core, t, out):
    nc = core.nc
    with ExitStack() as ctx:
        stored = core.sem("stored")
        block = ctx.enter_context(nc.Block())

        @block.sync
        def _(sp):
            sp.dma_start(out.rearrange("o (t p) d -> p (o t) d", p=P), t.x[:, :, :]).then_inc(stored, 16)
            sp.wait_ge(stored, 16)


def build(nc, dram, out, stop=9):
    NAMES.clear()
    with ExitStack() as ctx:
        core = Core(nc, ctx)
        t = Tensors()
        t.x = sbuf(nc, ctx, "x", [P, TT, D])
        t.ident = sbuf(nc, ctx, "ident", [P, P])
        t.scale = sbuf(nc, ctx, "mod_scale", [P, 3, KC])
        t.shift = sbuf(nc, ctx, "mod_shift", [P, 3, KC])
        t.gate = sbuf(nc, ctx, "mod_gate", [P, 3, D])
        t.ada_ctx = ctx.enter_context(ExitStack())
        t.ada_acc = sbuf(nc, t.ada_ctx, "ada_acc", [P, 9 * D])
        with ExitStack() as first:
            t.meta = sbuf(nc, first, "meta", [NM, D])
            t.mix_norm = sbuf(nc, first, "mix_norm", [P, KC])
            t.mixed_scale = sbuf(nc, first, "mixed_scale", [P, KC])
            t.neg_lam = sbuf(nc, first, "neg_lam", [P, 1])
            t.c_col = sbuf(nc, first, "c_col", [P, KC])
            t.lb = sbuf(nc, first, "lb", [P, RH])
            t.one_lb = sbuf(nc, first, "one_lb", [P, RH])
            load_first(core, t, dram)
            t.tm = sbuf(nc, first, "tm", [P, 3, TT, BANK])
            t.tm_meta = sbuf(nc, first, "tm_meta", [NM, 2, BANK])
            with ExitStack() as mix:
                t.fm = sbuf(nc, mix, "fm", [P, 16, NT])
                with ExitStack() as proj:
                    feat = Parts(core, proj, "feat", [P, KC, NT])
                    norm_to_features(core, t.x, t.ident, feat, t.mix_norm, meta=t.meta[:, :])
                    first_projection(core, t, dram, feat)
                t.mixed = sbuf(nc, mix, "mixed", [P, TT, BANK])
                t.rec = sbuf(nc, mix, "rec", [P, TT, BANK])
                rotate_first(core, t, dram)
                first_attention(core, t, dram)
                with ExitStack() as gla:
                    t.qe = sbuf(nc, gla, "qe", [P, RH, NT])
                    t.kd = sbuf(nc, gla, "kd", [P, RH, NT])
                    t.e_last = sbuf(nc, gla, "e_last", [P, RH, NCH])
                    t.within = sbuf(nc, gla, "within", [SUB, RH, T])
                    gla_prepare(core, t, dram)
                    gla_scan(core, t, dram)
                first_merge(core, t, dram)
        with ExitStack() as peer:
            scores = sbuf(nc, peer, "scores", [P, TT * 2 * PH + 2, NK])
            with ExitStack() as ctx2:
                feat = Parts(core, ctx2, "peer_feat", [P, KC, T])
                ffn_norm = sbuf(nc, ctx2, "ffn_norm", [P, KC])
                keys = sbuf(nc, ctx2, "subkeys", [P, 2 * PH, NK])
                peer_load(core, dram, ffn_norm, keys, scores)
                norm_to_features(core, t.x, t.ident, feat, ffn_norm)
                query = sbuf(nc, ctx2, "query", [P, 2 * PH, T])
                peer_queries(core, t, dram, feat, query)
                peer_scores(core, t, dram, query, keys,
                            scores[:, 0:TT * 2 * PH, :].rearrange("p (t b) k -> p t b k", t=TT))
            hidden = sbuf(nc, peer, "hidden", [P, TT, D])
            norm_rows(core, t, dram["ffn_norm_w"], t.x, hidden)
            peer_experts(core, t, dram, hidden, scores)
        core.start_over()
        norm_rows(core, t, dram["final_norm_w"], t.x, t.x)
        modulation(core, t, dram)
        t.ada_ctx.close()
        swiglu(core, t, t.scale[:, 0, :], t.shift[:, 0, :], t.gate[:, 0, :], dram["ffn1_w_gate_2"],
               dram["ffn1_w_up_2"], dram["ffn1_w_down_2"][0])
        if stop > 3:
            second_mixer(core, t, dram)
        if stop > 4:
            swiglu(core, t, t.scale[:, 2, :], t.shift[:, 2, :], t.gate[:, 2, :], dram["ffn2_w_gate_2"],
                   dram["ffn2_w_up_2"], dram["ffn2_w_down_2"][0])
            norm_rows(core, t, dram["norm_final_2"], t.x, t.x)
        store(core, t, out)


def constants():
    i = np.arange(P)
    out = {"ident": np.eye(P, dtype=np.float32)}
    out["causal"] = np.where(i[None, :] <= i[:, None], 0.0, NEG).astype(np.float32)
    turn = np.zeros((P, P), np.float32)
    for d in range(P):
        base, r = d // AHD * AHD, d % AHD
        if r < AHD // 2:
            turn[base + r + AHD // 2, d] = -1.0
        else:
            turn[base + r - AHD // 2, d] = 1.0
    out["rope_turn"] = turn
    inv = (np.float32(10000.0) ** (-np.arange(0, AHD, 2, dtype=np.float32) / np.float32(AHD))).astype(np.float32)
    ang = (np.arange(NT, dtype=np.float32)[:, None] * inv[None, :]).astype(np.float32)
    ang = np.concatenate([ang] * 4, axis=1).T
    out["rope_cos"] = np.ascontiguousarray(np.cos(ang).astype(np.float32))
    out["rope_sin"] = np.ascontiguousarray(np.sin(ang).astype(np.float32))
    out["chunk_keep"] = np.broadcast_to((np.arange(NT) % SUB != 0).astype(np.float32), (P, NT)).copy()
    out["one_hot"] = np.broadcast_to(np.eye(SUB, dtype=np.float32), (P, SUB, SUB)).copy()
    out["chunk_keep2"] = np.broadcast_to((np.arange(T) % P != 0).astype(np.float32), (SH, T)).copy()
    inv2 = (np.float32(10000.0) ** (-np.arange(0, ROPE, 2, dtype=np.float32) / np.float32(ROPE))).astype(np.float32)
    out["rope_inv"] = np.concatenate([inv2, inv2])[:, None].copy()
    turn2 = np.zeros((ROPE, ROPE), np.float32)
    for d in range(ROPE):
        turn2[(d + ROPE // 2) % ROPE, d] = -1.0 if d < ROPE // 2 else 1.0
    out["rope_turn2"] = turn2
    out["pick"] = np.ascontiguousarray(np.broadcast_to(np.eye(SH, dtype=np.float32)[:, :, None], (SH, SH, P)))
    out["causal_t"] = (i[:, None] <= i[None, :]).astype(np.float32)
    out["step16"] = np.broadcast_to(np.arange(TOPK, dtype=np.float32), (P, TOPK)).copy()
    return out


def feature_blocks(w, width=P):
    k, n = w.shape
    return np.ascontiguousarray(w.reshape(k // P, P, n // width, width).transpose(2, 1, 0, 3)
                                .reshape(n // width, P, k // P * width))


def column_blocks(w, width=BANK):
    k, n = w.shape
    return np.ascontiguousarray(w.reshape(k // P, P, n // width, width).transpose(2, 1, 0, 3))


def columns(v):
    return np.ascontiguousarray(v.reshape(-1, P).T)


def lay_out(inputs):
    a = {name: np.ascontiguousarray(value) for name, value in inputs.items()}
    w = a.pop("w_in")[0]
    aq, ak, av, rq, rf, ri, rg = [w[:, i * 512:(i + 1) * 512] for i in range(7)]
    a["w_in_f"] = np.concatenate([feature_blocks(m) for m in (aq, ak, rq, rf)])
    a["w_in_t"] = np.concatenate([column_blocks(m) for m in (av, ri, rg)])
    a["w_out_t"] = column_blocks(a.pop("w_out")[0])
    for name in ("mix_norm_w", "rec_norm_w", "c_2"):
        a[name] = columns(a[name])
    a["rec_lb_logits"] = columns(a["rec_lb_logits"]).reshape(P, 2, RH)
    for name in ("norm_ffn1_2", "norm_mix_2", "norm_ffn2_2"):
        a[name] = columns(a[name])
    a["norms_2"] = np.stack([a.pop("norm_ffn1_2"), a.pop("norm_mix_2"), a.pop("norm_ffn2_2")], axis=1)
    for name in ("ffn1_w_gate_2", "ffn1_w_up_2", "ffn2_w_gate_2", "ffn2_w_up_2"):
        a[name] = feature_blocks(a[name][0])
    w = a.pop("w_in_2")[0]
    z, conv, dt, cq, ckv, rope = np.split(w, [1024, 2560, 2576, 2960, 3216], axis=1)
    a["w_conv"] = feature_blocks(conv)
    a["w_z0"], a["w_z1"] = column_blocks(z)
    a["w_cq"], a["w_ckv"] = column_blocks(cq, QL)[0], column_blocks(ckv, KVL)[0]
    small = np.zeros((D, P), np.float32)
    small[:, 0:SH], small[:, NOPE:QKD] = dt, rope
    a["w_small"] = feature_blocks(small)
    a["conv_w_2"] = np.ascontiguousarray(a["conv_w_2"][0].reshape(4, 12, P).transpose(2, 0, 1))
    a["conv_b_2"] = columns(a["conv_b_2"])
    a["ssd_heads"] = np.ascontiguousarray(np.concatenate([a.pop("dt_bias_2"), a.pop("a_log_2")]).T)
    a["w_uq_2"] = np.ascontiguousarray(feature_blocks(a["w_uq_2"][0], QKD).transpose(1, 0, 2))
    ukv = a.pop("w_ukv_2")[0].reshape(KVL, MH, NOPE + MV)
    a["w_uk"] = np.ascontiguousarray(feature_blocks(ukv[:, :, :NOPE].reshape(KVL, MH * NOPE), NOPE).transpose(1, 0, 2))
    a["w_uv"] = np.ascontiguousarray(column_blocks(ukv[:, :, NOPE:].reshape(KVL, MH * MV)).transpose(1, 0, 2, 3))
    a["latent_norm"] = np.concatenate([columns(a.pop("q_norm_w_2")), columns(a.pop("kv_norm_w_2"))], axis=1)
    a["mix_norm_2"] = np.concatenate([columns(a.pop("ssd_norm_w_2")), columns(a.pop("mla_norm_w_2"))], axis=1)
    a["norm_final_2"] = a["norm_final_2"].reshape(1, D)
    a["peer_w_query"] = feature_blocks(a["peer_w_query"][0])
    a["peer_subkeys"] = np.ascontiguousarray(a["peer_subkeys"][0].reshape(2 * PH, NK, P).transpose(2, 0, 1))
    a["ffn_norm_cols"] = columns(a["ffn_norm_w"])
    a["final_norm_w"] = a["final_norm_w"].reshape(1, D)
    a["peer_table"] = np.concatenate([a.pop("peer_u")[0], a.pop("peer_v")[0]], axis=1)
    a["diff_subln_w"] = np.repeat(columns(a["diff_subln_w"]), AH, axis=1)
    return a


def kernel(**inputs):
    import concourse.bacc as bacc
    from concourse.bass_utils import run_bass_kernel_spmd

    nc = bacc.Bacc("TRN2", target_bir_lowering=False, num_devices=1)
    arrays = {**lay_out(inputs), **constants()}
    dram = {}
    for name, a in arrays.items():
        dram[name] = nc.dram_tensor(f"in_{name}", a.shape, mybir.dt.from_np(a.dtype), kind="ExternalInput").ap()
    out = nc.dram_tensor("out_0", (1, T, D), F32, kind="ExternalOutput").ap()
    build(nc, dram, out)
    result = run_bass_kernel_spmd(nc, [{f"in_{name}": a for name, a in arrays.items()}], core_ids=[0])
    return result.results[0]["out_0"]
```
